# Optimizing a Trainium2 kernel written in Bass

```python
import math
import jax, jax.numpy as jnp
from jax import lax
import numpy as np

D_MODEL = 1024
BATCH = 1
SEQ = 256
DEPTH = 1

HEAD_DIM = 64
N_HEADS = D_MODEL // HEAD_DIM
MOBA_HEADS = N_HEADS // 2
DIL_HEADS = N_HEADS - MOBA_HEADS
MOBA_WIDTH = MOBA_HEADS * HEAD_DIM
DIL_WIDTH = DIL_HEADS * HEAD_DIM
MIX_WIDTH = MOBA_WIDTH + DIL_WIDTH
IN_WIDTH = 3 * MIX_WIDTH
MOBA_BLOCK = 256
MOBA_TOPK = 3
MOBA_Q_CHUNK = 32
DIL_PAIRS = ((128, 1), (512, 4), (2048, 16))
DIL_BLOCK = 128
REL_BUCKETS = 32
REL_MAX_EXACT = 16
REL_MAX_DIST = 2048
PEER_HEADS = 8
PEER_N_KEYS = 128
PEER_N_EXPERTS = PEER_N_KEYS * PEER_N_KEYS
PEER_TOPK = 16
PEER_DK = 128
PEER_CHUNK = 128
DEEPNORM_ALPHA = (2 * DEPTH) ** 0.25
DEEPNORM_BETA = (8 * DEPTH) ** -0.25
LN_EPS = 1e-5
NEG_INF = -1e30

kernel_name = "hybrid_moba_dilated_peer_block"

def layer_norm(x, g, b):
    xf = x.astype(jnp.float32)
    mu = xf.mean(-1, keepdims=True)
    var = jnp.square(xf - mu).mean(-1, keepdims=True)
    return ((xf - mu) * lax.rsqrt(var + LN_EPS) * g + b).astype(x.dtype)

def rms_norm(x, g):
    xf = x.astype(jnp.float32)
    return (xf * lax.rsqrt(jnp.square(xf).mean(-1, keepdims=True) + LN_EPS) * g).astype(x.dtype)

def t5_bucket(dist):
    n = jnp.maximum(dist, 0)
    nf = jnp.maximum(n, 1).astype(jnp.float32)
    large = REL_MAX_EXACT + (jnp.log(nf / REL_MAX_EXACT) / math.log(REL_MAX_DIST / REL_MAX_EXACT)
                             * (REL_BUCKETS - REL_MAX_EXACT)).astype(jnp.int32)
    large = jnp.minimum(large, REL_BUCKETS - 1)
    return jnp.where(n < REL_MAX_EXACT, n, large)

def moba_attention(q, k, v, bias_tab):
    B, H, S, hd = q.shape
    nb = -(-S // MOBA_BLOCK)
    Sp = nb * MOBA_BLOCK
    pad = ((0, 0), (0, 0), (0, Sp - S), (0, 0))
    kp, vp = jnp.pad(k, pad), jnp.pad(v, pad)
    kblk = kp.reshape(B, H, nb, MOBA_BLOCK, hd)
    vblk = vp.reshape(B, H, nb, MOBA_BLOCK, hd)
    kmean = kblk.astype(jnp.float32).mean(3)
    qblk = jnp.arange(S) // MOBA_BLOCK
    gate = jnp.einsum('bhsd,bhnd->bhsn', q.astype(jnp.float32), kmean)
    past = jnp.arange(nb)[None, :] < qblk[:, None]
    gate = jnp.where(past, gate, -jnp.inf)
    k_sel = min(MOBA_TOPK, nb)
    _, sel = lax.top_k(gate, k_sel)
    sel_valid = jnp.arange(k_sel)[None, :] < qblk[:, None]
    scale = hd ** -0.5
    bi = jnp.arange(B)[:, None, None, None]
    hi = jnp.arange(H)[None, :, None, None]
    hi5 = jnp.arange(H)[None, :, None, None, None]

    def chunk(ci):
        t0 = ci * MOBA_Q_CHUNK
        qc = lax.dynamic_slice_in_dim(q, t0, MOBA_Q_CHUNK, 2)
        selc = lax.dynamic_slice_in_dim(sel, t0, MOBA_Q_CHUNK, 2)
        validc = lax.dynamic_slice_in_dim(sel_valid, t0, MOBA_Q_CHUNK, 0)
        qpos = t0 + jnp.arange(MOBA_Q_CHUNK)
        ks = kblk[bi, hi, selc]
        vs = vblk[bi, hi, selc]
        l_sel = jnp.einsum('bhqd,bhqkjd->bhqkj', qc, ks).astype(jnp.float32) * scale
        kpos_sel = selc[..., None] * MOBA_BLOCK + jnp.arange(MOBA_BLOCK)
        l_sel = l_sel + bias_tab[hi5, t5_bucket(qpos[:, None, None] - kpos_sel)]
        l_sel = jnp.where(validc[None, None, :, :, None], l_sel, NEG_INF)
        own0 = (t0 // MOBA_BLOCK) * MOBA_BLOCK
        ko = lax.dynamic_slice_in_dim(kp, own0, MOBA_BLOCK, 2)
        vo = lax.dynamic_slice_in_dim(vp, own0, MOBA_BLOCK, 2)
        dist = qpos[:, None] - (own0 + jnp.arange(MOBA_BLOCK))[None, :]
        l_own = jnp.einsum('bhqd,bhjd->bhqj', qc, ko).astype(jnp.float32) * scale
        l_own = jnp.where(dist >= 0, l_own + bias_tab[:, t5_bucket(dist)], NEG_INF)
        n_sel = k_sel * MOBA_BLOCK
        p = jax.nn.softmax(jnp.concatenate(
            [l_sel.reshape(B, H, MOBA_Q_CHUNK, n_sel), l_own], -1), axis=-1).astype(v.dtype)
        p_sel = p[..., :n_sel].reshape(B, H, MOBA_Q_CHUNK, k_sel, MOBA_BLOCK)
        return (jnp.einsum('bhqkj,bhqkjd->bhqd', p_sel, vs)
                + jnp.einsum('bhqj,bhjd->bhqd', p[..., n_sel:], vo))

    outs = lax.map(chunk, jnp.arange(S // MOBA_Q_CHUNK))
    return outs.transpose(1, 2, 0, 3, 4).reshape(B, H, S, hd)

def dilated_branch(q, k, v, bias_tab, window, dil):
    B, H, S, hd = q.shape
    L = S // dil
    nblk = -(-L // DIL_BLOCK)
    Lp = nblk * DIL_BLOCK

    def to_blocks(a):
        a = a.reshape(B, H, L, dil, hd).transpose(0, 1, 3, 2, 4)
        a = jnp.pad(a, ((0, 0), (0, 0), (0, 0), (0, Lp - L), (0, 0)))
        return a.reshape(B, H, dil, nblk, DIL_BLOCK, hd)

    qb, kb, vb = to_blocks(q), to_blocks(k), to_blocks(v)
    pad_prev = ((0, 0), (0, 0), (0, 0), (1, 0), (0, 0), (0, 0))
    k2 = jnp.concatenate([jnp.pad(kb, pad_prev)[:, :, :, :-1], kb], axis=4)
    v2 = jnp.concatenate([jnp.pad(vb, pad_prev)[:, :, :, :-1], vb], axis=4)
    logits = jnp.einsum('bhrnqd,bhrnkd->bhrnqk', qb, k2).astype(jnp.float32) * hd ** -0.5
    i = jnp.arange(DIL_BLOCK)[:, None]
    j = jnp.arange(2 * DIL_BLOCK)[None, :]
    off = DIL_BLOCK + i - j
    band = (off >= 0) & (off <= window // dil)
    has_prev = (jnp.arange(nblk)[:, None, None] > 0) | (j[None] >= DIL_BLOCK)
    mask = band[None] & has_prev
    bias = bias_tab[:, t5_bucket(off * dil)]
    logits = jnp.where(mask, logits + bias[:, None, None], NEG_INF)
    lse = jax.nn.logsumexp(logits, axis=-1)
    p = jnp.exp(logits - lse[..., None]).astype(v.dtype)
    o = jnp.einsum('bhrnqk,bhrnkd->bhrnqd', p, v2)
    o = o.reshape(B, H, dil, Lp, hd)[:, :, :, :L].transpose(0, 1, 3, 2, 4).reshape(B, H, S, hd)
    lse = lse.reshape(B, H, dil, Lp)[..., :L].transpose(0, 1, 3, 2).reshape(B, H, S)
    return o, lse

def dilated_attention(q, k, v, bias_tab):
    outs, lses = [], []
    for window, dil in DIL_PAIRS:
        o, l = dilated_branch(q, k, v, bias_tab, window, dil)
        outs.append(o)
        lses.append(l)
    wts = jax.nn.softmax(jnp.stack(lses, 0), axis=0)
    out = jnp.einsum('nbhs,nbhsd->bhsd', wts, jnp.stack(outs, 0).astype(jnp.float32))
    return out.astype(q.dtype)

def peer_ffn(h, w_q, sub_keys, u_tab, v_tab):
    B, S, D = h.shape
    T = B * S
    xt = h.reshape(T, D)
    q = (xt @ w_q).reshape(T, PEER_HEADS, PEER_DK)
    half = PEER_DK // 2
    s1 = jnp.einsum('thd,nd->thn', q[..., :half], sub_keys[0]).astype(jnp.float32)
    s2 = jnp.einsum('thd,nd->thn', q[..., half:], sub_keys[1]).astype(jnp.float32)
    v1, i1 = lax.top_k(s1, PEER_TOPK)
    v2, i2 = lax.top_k(s2, PEER_TOPK)
    cand = (v1[..., :, None] + v2[..., None, :]).reshape(T, PEER_HEADS, PEER_TOPK * PEER_TOPK)
    vals, pos = lax.top_k(cand, PEER_TOPK)
    e = (jnp.take_along_axis(i1, pos // PEER_TOPK, -1) * PEER_N_KEYS
         + jnp.take_along_axis(i2, pos % PEER_TOPK, -1))
    g = jax.nn.softmax(vals, axis=-1).astype(h.dtype)
    nc = T // PEER_CHUNK

    def chunk(args):
        xc, ec, gc = args
        pre = jnp.einsum('cd,chkd->chk', xc, u_tab[ec])
        a = jax.nn.gelu(pre, approximate=False) * gc
        return jnp.einsum('chk,chkd->cd', a, v_tab[ec])

    out = lax.map(chunk, (xt.reshape(nc, PEER_CHUNK, D),
                          e.reshape(nc, PEER_CHUNK, PEER_HEADS, PEER_TOPK),
                          g.reshape(nc, PEER_CHUNK, PEER_HEADS, PEER_TOPK)))
    return out.reshape(B, S, D)

def setup_inputs(seed: int = 0) -> dict:
    key = jax.random.key(seed)
    ks = jax.random.split(key, 17)
    f32 = jnp.float32

    def nrm(k, shape, s):
        return jax.random.normal(k, shape, f32) * s

    beta = DEEPNORM_BETA
    col_scale = jnp.concatenate([
        jnp.ones((2 * MOBA_WIDTH,), f32), jnp.full((MOBA_WIDTH,), beta, f32),
        jnp.ones((2 * DIL_WIDTH,), f32), jnp.full((DIL_WIDTH,), beta, f32)])
    return {
        "x": nrm(ks[0], (BATCH, SEQ, D_MODEL), 1.0),
        "c": nrm(ks[1], (BATCH, D_MODEL), 1.0),
        "w_ada": nrm(ks[2], (DEPTH, D_MODEL, 6 * D_MODEL), 0.2 * D_MODEL ** -0.5),
        "b_ada": nrm(ks[3], (DEPTH, 6 * D_MODEL), 0.01),
        "w_in": nrm(ks[4], (DEPTH, D_MODEL, IN_WIDTH), D_MODEL ** -0.5) * col_scale,
        "rel_bias": nrm(ks[5], (N_HEADS, REL_BUCKETS), 0.2),
        "gn_moba": 1.0 + nrm(ks[6], (DEPTH, MOBA_WIDTH), 0.02),
        "gn_dil": 1.0 + nrm(ks[7], (DEPTH, DIL_WIDTH), 0.02),
        "w_out": nrm(ks[8], (DEPTH, MIX_WIDTH, D_MODEL), beta * MIX_WIDTH ** -0.5),
        "ln1_g": 1.0 + nrm(ks[9], (DEPTH, D_MODEL), 0.02),
        "ln1_b": nrm(ks[10], (DEPTH, D_MODEL), 0.02),
        "w_q_peer": nrm(ks[11], (DEPTH, D_MODEL, PEER_HEADS * PEER_DK), D_MODEL ** -0.5),
        "sub_keys": nrm(ks[12], (DEPTH, 2, PEER_N_KEYS, PEER_DK // 2), (PEER_DK // 2) ** -0.5),
        "peer_u": nrm(ks[13], (DEPTH, PEER_N_EXPERTS, D_MODEL), beta * D_MODEL ** -0.5),
        "peer_v": nrm(ks[14], (DEPTH, PEER_N_EXPERTS, D_MODEL), beta),
        "ln2_g": 1.0 + nrm(ks[15], (DEPTH, D_MODEL), 0.02),
        "ln2_b": nrm(ks[16], (DEPTH, D_MODEL), 0.02),
    }

def reference(x, c, w_ada, b_ada, w_in, rel_bias, gn_moba, gn_dil, w_out, ln1_g, ln1_b,
              w_q_peer, sub_keys, peer_u, peer_v, ln2_g, ln2_b):
    B, S, D = x.shape
    bias_moba = rel_bias[:MOBA_HEADS]
    bias_dil = rel_bias[MOBA_HEADS:]
    c_act = jax.nn.silu(c)

    def heads(a, n):
        return a.reshape(B, S, n, HEAD_DIM).transpose(0, 2, 1, 3)

    for l in range(DEPTH):
        mod = c_act @ w_ada[l] + b_ada[l]
        sh1, sc1, g1, sh2, sc2, g2 = [m[:, None, :] for m in jnp.split(mod, 6, axis=-1)]
        h = x * (1 + sc1) + sh1
        proj = h @ w_in[l]
        qa, ka, va, qb, kb, vb = jnp.split(
            proj, np.cumsum([MOBA_WIDTH] * 3 + [DIL_WIDTH] * 2).tolist(), axis=-1)
        ya = moba_attention(heads(qa, MOBA_HEADS), heads(ka, MOBA_HEADS), heads(va, MOBA_HEADS), bias_moba)
        yb = dilated_attention(heads(qb, DIL_HEADS), heads(kb, DIL_HEADS), heads(vb, DIL_HEADS), bias_dil)
        ya = rms_norm(ya.transpose(0, 2, 1, 3).reshape(B, S, MOBA_WIDTH), gn_moba[l])
        yb = rms_norm(yb.transpose(0, 2, 1, 3).reshape(B, S, DIL_WIDTH), gn_dil[l])
        y = jnp.concatenate([ya, yb], axis=-1) @ w_out[l]
        x = layer_norm(DEEPNORM_ALPHA * x + (1 + g1) * y, ln1_g[l], ln1_b[l])
        h2 = x * (1 + sc2) + sh2
        f = peer_ffn(h2, w_q_peer[l], sub_keys[l], peer_u[l], peer_v[l])
        x = layer_norm(DEEPNORM_ALPHA * x + (1 + g2) * f, ln2_g[l], ln2_b[l])
    return x


_drawn_inputs = setup_inputs


def setup_inputs(seed=0):
    import zlib

    import numpy as np

    out = dict(_drawn_inputs(seed))
    spreads = {}
    factors = {'gn_moba': 11.416, 'gn_dil': 12.071, 'ln2_g': 8.351, 'ln2_b': 8.225}
    for name, (base, spread) in spreads.items():
        noise = np.random.default_rng([zlib.crc32(name.encode()), seed]).standard_normal(out[name].shape)
        drawn = base * np.exp(spread * noise) if base else spread * noise
        out[name] = __import__('jax').numpy.asarray(drawn.astype(out[name].dtype))
    for name, factor in factors.items():
        out[name] = (out[name] * factor).astype(out[name].dtype)
    return out
```

```python
import math
from contextlib import ExitStack

import numpy as np
import concourse.bass as bass
from concourse import mybir

F32 = mybir.dt.float32
I32 = mybir.dt.int32
U32 = mybir.dt.uint32
ALU = mybir.AluOpType
ACT = mybir.ActivationFunctionType
AX = mybir.AxisListType

P = 128
D = 1024
T = 256
NT = T // P
KC = D // P
HD = 64
NH = 16
CH = 512
BUCKETS = 32
ROW = 384
MASKED = -1e30
ALPHA = 2.0 ** 0.25
EPS = 1e-5
SCALE = HD ** -0.5
PH = 8
NK = 128
TOPK = 16
SLOTS = PH * TOPK
PAIR = 2 * TOPK
TURNS = SLOTS // PAIR
RING = 8
WRING = 4
TAKEN = -3e38
DIAGS = 4

STREAM = [("ada", 0), ("ada", 1), ("ada", 2), ("ada", 3), ("in", 0), ("in", 1), ("in", 2), ("ada", 4), ("in", 3),
          ("ada", 5), ("ada", 6), ("in", 4), ("ada", 7), ("ada", 8), ("in", 5), ("ada", 9), ("ada", 10), ("ada", 11),
          ("out", 0), ("out", 1), ("q", 0), ("q", 1)]
G1, SH2, SC2, G2 = range(4)
UNITS = [(t, g, par, half) for g in range(2) for t, par, half in
         [(0, 0, 0), (0, 1, 0), (1, 0, 0), (1, 0, 1), (1, 1, 0), (1, 1, 1)]]
PLAN = (
    [("bias",), ("modc",), ("qk", 0, 0), ("qk", 0, 1), ("qk", 1, 0), ("qk", 1, 1)]
    + [("tflip", j) for j in range(4)]
    + [("S", 0), ("S", 1), ("v", 0, 0), ("v", 0, 1), ("Tr", 0), ("modrow", 0), ("qk", 2, 0), ("PV", 0), ("Tr", 1),
       ("S", 2), ("qk", 2, 1), ("modrow", 1), ("PV", 1), ("Tr", 2), ("S", 3), ("modrow", 2), ("qk", 3, 0), ("PV", 2),
       ("Tr", 3), ("S", 4), ("modrow", 3), ("qk", 3, 1), ("PV", 3), ("Tr", 4), ("S", 5)]
    + [("tflip", j) for j in range(4, 8)]
    + [("modrow", 4), ("PV", 4), ("Tr", 5), ("v", 1, 0), ("PV", 5), ("v", 1, 1), ("modrow", 5),
       ("S", 6), ("S", 7), ("modrow", 6), ("Tr", 6), ("S", 8), ("PV", 6), ("Tr", 7), ("S", 9), ("PV", 7), ("ny", 0),
       ("modrow", 7), ("Tr", 8), ("S", 10), ("PV", 8), ("yT", 0, 0), ("yT", 0, 1), ("Tr", 9), ("S", 11), ("PV", 9),
       ("wo", 0, 0), ("Tr", 10), ("PV", 10), ("wo", 0, 1), ("Tr", 11), ("PV", 11), ("rows2",), ("ln1", 0), ("ny", 1),
       ("yT", 1, 0), ("yT", 1, 1), ("wo", 1, 0), ("hT", 0, 0), ("hT", 0, 1), ("wo", 1, 1),
       ("q", 0, 0), ("s", 0, 0, 0), ("s", 0, 0, 1), ("route",), ("q", 0, 1), ("s", 0, 1, 0), ("s", 0, 1, 1),
       ("ln1", 1), ("hT", 1, 0), ("hT", 1, 1), ("q", 1, 0), ("q", 1, 1),
       ("s", 1, 0, 0), ("s", 1, 0, 1), ("s", 1, 1, 0), ("s", 1, 1, 1)]
)
for _m in range(8):
    PLAN.insert(PLAN.index(("modrow", _m)) + 3, ("madd", _m))
CHUNK = {key: n for n, key in enumerate(STREAM)}
STEP_BANKS = 6
NO_FILL = ("ny", "ln1", "route", "rows2", "madd")
FILLS = [s for s in PLAN if s[0] not in NO_FILL]
LATE = [("wo", 1, 0), ("wo", 1, 1)]
PLACE = {s: (n % STEP_BANKS, n // STEP_BANKS) for n, s in enumerate(s for s in FILLS if s not in LATE)}
PLACE |= {s: (STEP_BANKS + n, 0) for n, s in enumerate(LATE)}


def unit_heads(u):
    t, g, par, half = UNITS[u]
    b0, n = (0, 4) if t == 0 else (2 * half, 2)
    return b0, n, 8 * g + 4 * par + b0


class Steps:

    def __init__(self, eng, sem):
        self.eng, self.sem, self.n = eng, sem, 0

    def then(self, ins):
        ins.then_inc(self.sem, 1)
        self.n = self.n + 1

    def settle(self):
        self.eng.wait_ge(self.sem, self.n)

    def settle_here(self, gate):
        self.settle()
        self.eng.sem_inc(gate, 1)


def build(nc, A, out):
    ctx = ExitStack()
    with ctx:
        def sb(name, shape, dt=F32):
            return ctx.enter_context(nc.sbuf_tensor(name, shape, dt))

        def sem(name):
            return ctx.enter_context(nc.semaphore(name))

        ring = sb("ring", [P, RING, 2 * D])
        wring = ring[:].rearrange("p r c -> p (r c)").rearrange("p (w k n) -> p w k n", w=WRING, k=KC)
        xT_y = sb("xT_y", [P, KC * T])
        xT = xT_y[:].rearrange("p (k t) -> p k t", k=KC)
        y = xT_y[:].rearrange("p (t c) -> p t c", t=NT)
        hT_yT = sb("hT_yT", [P, KC * T])
        hT = hT_yT[:].rearrange("p (k t) -> p k t", k=KC)
        yT = hT_yT[:].rearrange("p (t k c) -> p t k c", t=NT, k=KC)
        x = sb("x", [P, NT, D])
        QT_h2T = sb("QT_h2T", [P, KC * T])
        QT = QT_h2T[:].rearrange("p (b t) -> p b t", b=KC)
        h2T = QT_h2T[:].rearrange("p (t k c) -> p t k c", t=NT, k=KC)
        KT_qT = sb("KT_qT", [P, KC * T])
        KT = KT_qT[:].rearrange("p (b t) -> p b t", b=KC)
        qT = KT_qT[:].rearrange("p (t h c) -> p t h c", t=NT, h=PH)
        V_x1 = sb("V_x1", [P, NT, D])
        H_s = sb("H_s", [P, NH * T])
        hankel = H_s[:].rearrange("p (h k) -> p h k", h=NH)
        scores = H_s[:].rearrange("p (t h z n) -> p t h z n", t=NT, h=PH, z=2)
        T_h2 = sb("T_h2", [P, NH * T])
        toep = T_h2[:].rearrange("p (h k) -> p h k", h=NH)
        h2 = T_h2[:, 0:NT * D].rearrange("p (t c) -> p t c", t=NT)
        mod = sb("mod", [P, 4, D])
        lnw = sb("lnw", [P, 4, D])
        acc = sb("acc", [P, 2, CH])
        prob = sb("prob", [P, 2, CH])
        probT = sb("probT", [P, 2, CH])
        onehot = probT[0:BUCKETS, 0, 0:ROW]
        maskrow = probT[0:NH, 1, 0:ROW]
        biasrow = prob[0:NH, 0, 0:ROW]
        relT = sb("relT", [BUCKETS, NH])
        consts = sb("consts", [P, 2 * P + TOPK])
        ident, flip, iota = consts[:, 0:P], consts[:, P:2 * P], consts[:, 2 * P:2 * P + TOPK]
        ones = sb("ones", [P, P])
        zeros = sb("zeros", [P, CH])
        cin = sb("cin", [P, KC])
        ctanh = sb("ctanh", [P, KC])
        cact = sb("cact", [P, KC])
        badac = sb("badac", [P, 2 * KC])
        modc = sb("modc", [P, 2 * KC])
        gn = sb("gn", [P, KC])
        skT = sb("skT", [P, NK])
        epsc = sb("epsc", [P, 1])
        negmax = sb("negmax", [P, len(UNITS), 4])
        psum_p = sb("psum_p", [P, len(UNITS), 4])
        prec = sb("prec", [P, len(UNITS), 4])
        ystat = sb("ystat", [P, NT, 3, 2])
        lnst = sb("lnst", [P, 2 * NT, 6])
        junk = sb("junk", [P, D], mybir.dt.bfloat16)
        diag = sb("diag", [P, DIAGS, P])
        swork = sb("swork", [P, 2, 2, NK])
        v16 = sb("v16", [P, 2, TOPK])
        i16 = sb("i16", [P, 2, TOPK], U32)
        cand = sb("cand", [P, 2, TOPK * TOPK])
        best = sb("best", [P, TOPK])
        pos = sb("pos", [P, TOPK], U32)
        pij = sb("pij", [P, 2, TOPK], U32)
        eq = sb("eq", [P, 2, TOPK, TOPK])
        eij = sb("eij", [P, 2, TOPK])
        esum = sb("esum", [P, TOPK])
        bdiff = sb("bdiff", [P, TOPK])
        bexp = sb("bexp", [P, TOPK])
        bsum = sb("bsum", [P, 2])
        e_all = sb("e_all", [P, NT * SLOTS], I32)
        g_all = sb("g_all", [P, NT * SLOTS])
        pre = sb("pre", [P, PAIR])
        gel = sb("gel", [P, PAIR])
        idx = sb("idx", [P, 2, TOPK], I32)
        bank = [ctx.enter_context(nc.psum_tensor(f"bank{i}", [P, CH], F32))[:] for i in range(STEP_BANKS)]
        fsum = ctx.enter_context(nc.psum_tensor("fsum", [P, 2, CH], F32))
        bank += [fsum[:, 0, :], fsum[:, 1, :]]

        bank_full = [sem(f"bank_full{i}") for i in range(len(bank))]
        bank_free = [sem(f"bank_free{i}") for i in range(len(bank))]
        w_in = [sem(f"w_in{i}") for i in range(WRING)]
        modc_part = sem("modc_part")
        c_in, bias_in, xT_in, consts_in, x_in, rows_in, gnsk_in = (sem(n) for n in (
            "c_in", "bias_in", "xT_in", "consts_in", "x_in", "rows_in", "gnsk_in"))
        biasrow_out, hankel_in = sem("biasrow_out"), sem("hankel_in")
        tanh_ready, cact_ready, hT_ready = sem("tanh_ready"), sem("cact_ready"), sem("hT_ready")
        acc_ready = sem("acc_ready")
        negmax_ready, exp_ready = sem("negmax_ready"), sem("exp_ready")
        sq_ready, y_normed = sem("sq_ready"), sem("y_normed")
        mean_ready, std_ready = sem("mean_ready"), sem("std_ready")
        normed_ready, x1_ready, h2_ready, rows2_ready = sem("normed_ready"), sem("x1_ready"), sem("h2_ready"), sem("rows2_ready")
        set_ready = sem("set_ready")
        dve_step, act_step, pool_step = sem("dve_step"), sem("act_step"), sem("pool_step")
        dve_gate, pool_gate = sem("dve_gate"), sem("pool_gate")
        best_ready, bexp_ready, e_ready = sem("best_ready"), sem("bexp_ready"), sem("e_ready")
        idx_staged = sem("idx_staged")
        slot_in = [sem(f"slot_in{i}") for i in range(RING)]
        slot_free = sem("slot_free")
        dots_ready, gelu_ready, diag_ready = sem("dots_ready"), sem("gelu_ready"), sem("diag_ready")
        f_ready, f_taken, out_ready, out_done = sem("f_ready"), sem("f_taken"), sem("out_ready"), sem("out_done")

        def filled(eng, step):
            b, n = PLACE[step]
            eng.wait_ge(bank_full[b], n + 1)
            return bank[b]

        def freed(step):
            return bank_free[PLACE[step][0]]

        def settle_bank(eng, step):
            b, n = PLACE[step]
            eng.wait_ge(bank_free[b], n + 1)

        def chunk(eng, key):
            n = CHUNK[key]
            eng.wait_ge(w_in[n % WRING], 16 * (n // WRING + 1))
            return wring[:, n % WRING]

        def chunk_used(eng, key):
            m, c = key
            if key == ("ada", 3):
                filled(eng, ("modc",))
            elif m == "ada" and c < 3:
                eng.wait_ge(modc_part, c + 1)
            elif m == "ada":
                eng.wait_ge(acc_ready, c - 3)
            elif m == "in":
                filled(eng, (("qk", 0, 1), ("qk", 1, 1), ("v", 0, 1), ("qk", 2, 1), ("qk", 3, 1), ("v", 1, 1))[c])
            else:
                raise ValueError("nothing follows this chunk")

        block = ctx.enter_context(nc.Block())

        @block.sync
        def _(sp):
            sp.dma_start(cin[:], A["c"]).then_inc(c_in, 16)
            sp.dma_start(badac[:], A["b_ada_c"]).then_inc(c_in, 16)
            for name, dst in (("relT", relT[:]), ("onehot", onehot), ("maskrow", maskrow)):
                sp.dma_start(dst, A[name]).then_inc(bias_in, 16)
            sp.dma_start(consts[:], A["consts"]).then_inc(consts_in, 16)

            def load(n):
                if n >= WRING:
                    chunk_used(sp, STREAM[n - WRING])
                sp.dma_start(wring[:, n % WRING], A["w"][n].rearrange("p (k n) -> p k n", k=KC)).then_inc(w_in[n % WRING], 16)

            load(0)
            load(1)
            sp.dma_start(xT, A["xT"].rearrange("p (k t) -> p k t", k=KC)).then_inc(xT_in, 16)
            load(2)
            load(3)
            settle_bank(sp, ("bias",))
            sp.dma_start(A["scratch"], biasrow).then_inc(biasrow_out, 16)
            sp.wait_ge(biasrow_out, 16)
            shifts = bass.AP(A["scratch"].tensor, 0, [[1, P], [ROW, NH], [1, T]])
            sp.dma_start(hankel, shifts).then_inc(hankel_in, 16)
            for n in range(WRING, len(STREAM)):
                load(n)
                if n == 6:
                    sp.dma_start(mod[:].rearrange("p r c -> p (r c)"), A["b_ada_r"].broadcast_to([P, 4 * D])).then_inc(rows_in, 16)
                if n == 8:
                    sp.dma_start(x[:], A["x"].rearrange("(t p) c -> p t c", p=P)).then_inc(x_in, 16)
                    sp.dma_start(gn[:], A["gn"]).then_inc(gnsk_in, 16)
                    sp.dma_start(skT[:], A["skT"]).then_inc(gnsk_in, 16)
                if n == 10:
                    sp.dma_start(lnw[:].rearrange("p r c -> p (r c)"), A["ln"].broadcast_to([P, 4 * D])).then_inc(rows_in, 16)
            for t in range(NT):
                sp.wait_ge(out_ready, t + 1)
                sp.dma_start(out[0, P * t:P * t + P, :], V_x1[:, t, :]).then_inc(out_done, 16)
            sp.wait_ge(out_done, 16 * NT)

        @block.tensor
        def _(pe):
            def open_bank(step):
                b, n = PLACE[step]
                if n:
                    pe.wait_ge(bank_free[b], n)
                return bank[b], bank_full[b]

            def product(dst, lhs, rhs, n=KC):
                for k in range(n):
                    last = nc.tensor.matmul(dst, lhs(k), rhs(k), start=(k == 0), stop=(k == n - 1))
                return last

            for step in PLAN:
                kind = step[0]
                if kind in NO_FILL:
                    continue
                dst, full = open_bank(step)
                if kind == "bias":
                    pe.wait_ge(bias_in, 48)
                    nc.tensor.matmul(dst[0:NH, 0:ROW], relT[:], onehot, start=True, stop=True).then_inc(full, 1)
                elif kind == "modc":
                    pe.wait_ge(cact_ready, 1)
                    for c in range(4):
                        w = chunk(pe, ("ada", c))
                        for j in range(4):
                            last = product(dst[:, 4 * c + j:4 * c + j + 1], lambda k: w[:, k, P * j:P * j + P],
                                           lambda k: cact[:, k:k + 1])
                        last.then_inc(modc_part if c < 3 else full, 1)
                elif kind == "qk":
                    c, i = step[1:]
                    key = ("in", (0, 1, 3, 4)[c])
                    w = chunk(pe, key)
                    pe.wait_ge(hT_ready, 1)
                    for j in range(2):
                        last = product(dst[:, T * j:T * j + T], lambda k: w[:, k, P * (2 * i + j):P * (2 * i + j) + P],
                                       lambda k: hT[:, k, :])
                    last.then_inc(full, 1)
                elif kind == "v":
                    g, t = step[1:]
                    w = chunk(pe, ("in", 2 + 3 * g))
                    product(dst[:], lambda k: hT[:, k, P * t:P * t + P], lambda k: w[:, k, :]).then_inc(full, 1)
                elif kind == "tflip":
                    pe.wait_ge(consts_in, 16)
                    pe.wait_ge(hankel_in, 16)
                    nc.tensor.matmul(dst[:], flip, H_s[:, CH * step[1]:CH * step[1] + CH], start=True, stop=True).then_inc(full, 1)
                elif kind == "modrow":
                    pe.wait_ge(set_ready, 1)
                    pe.wait_ge(acc_ready, step[1] + 1)
                    nc.tensor.matmul(dst[:], ones[:], acc[:, step[1] % 2, :], start=True, stop=True).then_inc(full, 1)
                elif kind == "S":
                    t, g, par, half = UNITS[step[1]]
                    b0, n, _ = unit_heads(step[1])
                    for i in range(2):
                        settle_bank(pe, ("qk", 2 * g, i))
                        settle_bank(pe, ("qk", 2 * g + 1, i))
                    r = slice(HD * par, HD * par + HD)
                    keys = P * (t + 1)
                    for j in range(n):
                        last = nc.tensor.matmul(dst[:, keys * j:keys * j + keys], QT[r, 4 * g + b0 + j, P * t:P * t + P],
                                                KT[r, 4 * g + b0 + j, 0:keys], start=True, stop=True)
                    last.then_inc(full, 1)
                elif kind == "Tr":
                    pe.wait_ge(exp_ready, step[1] + 1)
                    pe.wait_ge(consts_in, 16)
                    for j in range(4):
                        last = nc.tensor.transpose(dst[:, P * j:P * j + P], prob[:, step[1] % 2, P * j:P * j + P], ident)
                    last.then_inc(full, 1)
                elif kind == "PV":
                    t, g, par, half = UNITS[step[1]]
                    b0, n, _ = unit_heads(step[1])
                    settle_bank(pe, ("Tr", step[1]))
                    for tt in range(t + 1):
                        settle_bank(pe, ("v", g, tt))
                    for j in range(n):
                        c = D // 2 * g + P * (b0 + j) + HD * par
                        for kt in range(t + 1):
                            at = P * ((t + 1) * j + kt)
                            last = nc.tensor.matmul(dst[:, HD * j:HD * j + HD], probT[:, step[1] % 2, at:at + P],
                                                    V_x1[:, kt, c:c + HD], start=(kt == 0), stop=(kt == t))
                    last.then_inc(full, 1)
                elif kind == "yT":
                    t, g = step[1:]
                    pe.wait_ge(y_normed, 2 * t + 2)
                    for j in range(4):
                        last = nc.tensor.transpose(dst[:, P * j:P * j + P], y[:, t, P * (4 * g + j):P * (4 * g + j) + P], ident)
                    last.then_inc(full, 1)
                elif kind == "wo":
                    t, n = step[1:]
                    w = chunk(pe, ("out", n))
                    settle_bank(pe, ("yT", t, 0))
                    settle_bank(pe, ("yT", t, 1))
                    product(dst[:], lambda k: yT[:, t, k, :], lambda k: w[:, k, :]).then_inc(full, 1)
                elif kind == "hT":
                    t, i = step[1:]
                    pe.wait_ge(h2_ready, t + 1)
                    for j in range(4):
                        last = nc.tensor.transpose(dst[:, P * j:P * j + P], h2[:, t, P * (4 * i + j):P * (4 * i + j) + P], ident)
                    last.then_inc(full, 1)
                elif kind == "q":
                    t, i = step[1:]
                    w = chunk(pe, ("q", i))
                    settle_bank(pe, ("hT", t, 0))
                    settle_bank(pe, ("hT", t, 1))
                    for j in range(4):
                        last = product(dst[:, P * j:P * j + P], lambda k: w[:, k, P * j:P * j + P], lambda k: h2T[:, t, k, :])
                    last.then_inc(full, 1)
                elif kind == "s":
                    t, i, z = step[1:]
                    pe.wait_ge(gnsk_in, 32)
                    settle_bank(pe, ("q", t, i))
                    r = slice(HD * z, HD * z + HD)
                    for j in range(4):
                        last = nc.tensor.matmul(dst[:, P * j:P * j + P], qT[r, t, 4 * i + j, :], skT[r, :], start=True, stop=True)
                    last.then_inc(full, 1)

            def slots(turn):
                for s in range(PAIR):
                    r = (s + RING // 2) % RING
                    pe.wait_ge(diag_ready, turn * PAIR + (s + 1))
                    for n in range(2):
                        last = nc.tensor.matmul(fsum[:, n, :], diag[:, s % DIAGS, :], ring[:, r, D + CH * n:D + CH * n + CH],
                                                start=False, stop=False)
                    last.then_inc(slot_free, 1)

            for step in LATE:
                settle_bank(pe, step)
            for t in range(NT):
                if t:
                    pe.wait_ge(f_taken, 2 * t)
                for n in range(2):
                    nc.tensor.matmul(fsum[:, n, :], zeros[:, 0:P], zeros[:], start=True, stop=False)
                with pe.Fori(TURNS * t, TURNS * (t + 1)) as turn:
                    slots(turn)
                for n in range(2):
                    last = nc.tensor.matmul(fsum[:, n, :], zeros[:, 0:P], zeros[:], start=False, stop=True)
                last.then_inc(f_ready, 1)

        @block.scalar
        def _(act):
            own = Steps(act, act_step)
            act.wait_ge(set_ready, 1)
            act.wait_ge(c_in, 32)
            nc.scalar.activation(ctanh[:], cin[:], ACT.Tanh, scale=0.5).then_inc(tanh_ready, 1)

            def route_exp(head):
                act.wait_ge(best_ready, head + 1)
                nc.scalar.activation(bexp[:], bdiff[:], ACT.Exp, accum_out=bsum[:, 0:1]).then_inc(bexp_ready, 1)

            def evacuate(step, dst, src):
                nc.scalar.copy(dst, src).then_inc(freed(step), 1)

            def deviation(i, z):
                act.wait_ge(mean_ready, i + 1)
                own.settle()
                own.then(nc.scalar.activation(junk[:], z, ACT.Square, bias=lnst[:, i, 2:3], accum_out=lnst[:, i, 3:4]))
                own.settle()
                nc.scalar.activation(lnst[:, i, 4:5], lnst[:, i, 3:4], ACT.Sqrt, bias=epsc[:], scale=1.0 / D).then_inc(std_ready, 1)

            for step in PLAN:
                kind = step[0]
                if kind == "tflip":
                    src = filled(act, step)
                    evacuate(step, T_h2[:, CH * step[1]:CH * step[1] + CH], src[:])
                elif kind == "qk":
                    c, i = step[1:]
                    dst = (QT, KT)[c % 2][:, 4 * (c // 2) + 2 * i:4 * (c // 2) + 2 * i + 2, :]
                    evacuate(step, dst, filled(act, step)[:].rearrange("p (j t) -> p j t", j=2))
                elif kind == "v":
                    g, t = step[1:]
                    evacuate(step, V_x1[:, t, CH * g:CH * g + CH], filled(act, step)[:])
                elif kind == "S":
                    t = UNITS[step[1]][0]
                    _, n, _ = unit_heads(step[1])
                    keys = P * (t + 1)
                    act.wait_ge(negmax_ready, step[1] + 1)
                    for j in range(n):
                        part = prob[:, step[1] % 2, keys * j:keys * j + keys]
                        last = nc.scalar.activation(part, part, ACT.Exp, bias=negmax[:, step[1], j:j + 1],
                                                    accum_out=psum_p[:, step[1], j:j + 1])
                    last.then_inc(exp_ready, 1)
                elif kind == "Tr":
                    if step[1] >= 2:
                        b, n = PLACE[("PV", step[1] - 2)]
                        act.wait_ge(bank_full[b], n + 1)
                    evacuate(step, probT[:, step[1] % 2, :], filled(act, step)[:])
                elif kind == "ny":
                    t = step[1]
                    for u, unit in enumerate(UNITS):
                        if unit[0] == t:
                            settle_bank(act, ("PV", u))
                    for g in range(2):
                        own.then(nc.scalar.activation(junk[:, 0:CH], y[:, t, CH * g:CH * g + CH], ACT.Square,
                                                      accum_out=ystat[:, t, 0, g:g + 1]))
                        own.settle()
                    nc.scalar.activation(ystat[:, t, 1, :], ystat[:, t, 0, :], ACT.Sqrt, bias=epsc[:],
                                         scale=1.0 / CH).then_inc(sq_ready, 1)
                elif kind == "ln1":
                    t = step[1]
                    deviation(t, x[:, t, :])
                elif kind == "hT":
                    t, i = step[1:]
                    evacuate(step, h2T[:, t, 4 * i:4 * i + 4, :], filled(act, step)[:].rearrange("p (j c) -> p j c", j=4))
                elif kind == "q":
                    t, i = step[1:]
                    evacuate(step, qT[:, t, 4 * i:4 * i + 4, :], filled(act, step)[:].rearrange("p (j c) -> p j c", j=4))
                    if step == ("q", 1, 1):
                        act.sem_inc(slot_free, RING // 2)
                elif kind == "s":
                    t, i, z = step[1:]
                    evacuate(step, scores[:, t, 4 * i:4 * i + 4, z, :], filled(act, step)[:].rearrange("p (j n) -> p j n", j=4))
                elif kind == "route":
                    for h in range(2):
                        route_exp(h)

            def gelus(turn, p0, p1):
                for p in range(p0, p1):
                    act.wait_ge(dots_ready, turn * (PAIR // 2) + (p + 1))
                    nc.scalar.activation(gel[:, 2 * p:2 * p + 2], pre[:, 2 * p:2 * p + 2], ACT.Gelu).then_inc(gelu_ready, 1)

            def turn_body(turn, routes):
                gelus(turn, 0, 4)
                if routes:
                    route_exp(2 * turn + 2)
                gelus(turn, 4, 12)
                if routes:
                    route_exp(2 * turn + 3)
                gelus(turn, 12, 16)

            with act.Fori(0, TURNS) as turn:
                turn_body(turn, True)
            deviation(NT, V_x1[:, 0, :])
            with act.Fori(TURNS, NT * TURNS - 1) as turn:
                turn_body(turn, True)
            turn_body(NT * TURNS - 1, False)
            deviation(NT + 1, V_x1[:, 1, :])

        @block.vector
        def _(dve):
            own = Steps(dve, dve_step)
            nc.vector.memset(ones[:], 1.0)
            nc.vector.memset(zeros[:], 0.0)
            nc.vector.memset(epsc[:], EPS).then_inc(set_ready, 1)

            def normalise(i, gate, f, res, z):
                for n in range(2):
                    src, ready, taken = f[n]
                    own.settle()
                    dve.wait_ge(*ready)
                    nc.vector.tensor_tensor(acc[:, n, :], src, gate[:, CH * n:CH * n + CH], ALU.mult).then_inc(taken[0], 1)
                    dve.wait_ge(*taken)
                    own.then(nc.vector.scalar_tensor_tensor(z[:, CH * n:CH * n + CH], res[:, CH * n:CH * n + CH], ALPHA,
                                                            acc[:, n, :], ALU.mult, ALU.add, accum_out=lnst[:, i, n:n + 1]))
                own.settle()
                nc.vector.tensor_scalar(lnst[:, i, 2:3], lnst[:, i, 0:1], lnst[:, i, 1:2], -1.0 / D,
                                        ALU.add, ALU.mult).then_inc(mean_ready, 1)

            def centre(i, z):
                dve.wait_ge(std_ready, i + 1)
                own.then(nc.vector.reciprocal(lnst[:, i, 5:6], lnst[:, i, 4:5]))
                own.settle()
                return nc.vector.tensor_scalar(z, z, lnst[:, i, 2:3], lnst[:, i, 5:6], ALU.add, ALU.mult)

            def route(turn, both, h):
                def settle():
                    own.settle_here(dve_gate)

                settle()
                own.then(nc.vector.tensor_copy(swork[:, 0], both))
                settle()
                for z in range(2):
                    own.then(nc.vector.max(v16[:, z, 0:8], swork[:, 0, z, :]))
                settle()
                for z in range(2):
                    own.then(nc.vector.max_index(i16[:, z, 0:8], v16[:, z, 0:8], swork[:, 0, z, :]))
                    own.then(nc.vector.match_replace(swork[:, 1, z, :], v16[:, z, 0:8], swork[:, 0, z, :], TAKEN))
                settle()
                for z in range(2):
                    own.then(nc.vector.max(v16[:, z, 8:16], swork[:, 1, z, :]))
                settle()
                for z in range(2):
                    own.then(nc.vector.max_index(i16[:, z, 8:16], v16[:, z, 8:16], swork[:, 1, z, :]))
                square = [P, TOPK, TOPK]
                own.then(nc.vector.tensor_tensor(cand[:, 0, :].rearrange("p (i j) -> p i j", i=TOPK),
                                                 v16[:, 0, :].unsqueeze(2).broadcast_to(square),
                                                 v16[:, 1, :].unsqueeze(1).broadcast_to(square), ALU.add))
                settle()
                own.then(nc.vector.max(best[:, 0:8], cand[:, 0, :]))
                settle()
                own.then(nc.vector.max_index(pos[:, 0:8], best[:, 0:8], cand[:, 0, :]))
                own.then(nc.vector.match_replace(cand[:, 1, :], best[:, 0:8], cand[:, 0, :], TAKEN))
                settle()
                own.then(nc.vector.max(best[:, 8:16], cand[:, 1, :]))
                settle()
                nc.vector.tensor_scalar(bdiff[:], best[:], best[:, 0:1], None, ALU.subtract).then_inc(best_ready, 1)
                own.then(nc.vector.max_index(pos[:, 8:16], best[:, 8:16], cand[:, 1, :]))
                settle()
                own.then(nc.vector.tensor_scalar(pij[:, 0, :], pos[:], 4, None, ALU.logical_shift_right))
                own.then(nc.vector.tensor_scalar(pij[:, 1, :], pos[:], TOPK - 1, None, ALU.bitwise_and))
                settle()
                cube = [P, 2, TOPK, TOPK]
                own.then(nc.vector.tensor_tensor(eq[:], pij[:].unsqueeze(3).broadcast_to(cube),
                                                 iota.unsqueeze(1).unsqueeze(1).broadcast_to(cube), ALU.is_equal))
                settle()
                own.then(nc.vector.tensor_tensor(eq[:], eq[:], i16[:].unsqueeze(2).broadcast_to(cube), ALU.mult))
                settle()
                own.then(nc.vector.tensor_reduce(eij[:], eq[:], AX.X, ALU.add))
                settle()
                own.then(nc.vector.scalar_tensor_tensor(esum[:], eij[:, 0, :], float(NK), eij[:, 1, :], ALU.mult, ALU.add))
                settle()
                at = turn * PAIR + TOPK * h
                here = bass.ds(at, TOPK)
                nc.vector.tensor_copy(e_all[:, here], esum[:]).then_inc(e_ready, 1)
                dve.wait_ge(bexp_ready, turn * 2 + (h + 1))
                own.then(nc.vector.reciprocal(bsum[:, 1:2], bsum[:, 0:1]))
                settle()
                own.then(nc.vector.tensor_scalar(g_all[:, here], bexp[:], bsum[:, 1:2], None, ALU.mult))
                settle()

            for step in PLAN:
                kind = step[0]
                if kind == "bias":
                    dve.wait_ge(bias_in, 48)
                    src = filled(dve, step)
                    nc.vector.tensor_tensor(biasrow, src[0:NH, 0:ROW], maskrow, ALU.add).then_inc(freed(step), 1)
                    dve.wait_ge(tanh_ready, 1)
                    own.then(nc.vector.tensor_scalar(ctanh[:], ctanh[:], 1.0, 0.5, ALU.add, ALU.mult))
                    own.settle()
                    nc.vector.tensor_tensor(cact[:], ctanh[:], cin[:], ALU.mult).then_inc(cact_ready, 1)
                elif kind == "modc":
                    src = filled(dve, step)
                    nc.vector.tensor_tensor(modc[:], src[:, 0:2 * KC], badac[:], ALU.add).then_inc(freed(step), 1)
                    settle_bank(dve, step)
                    own.then(nc.vector.tensor_scalar(modc[:, KC:], modc[:, KC:], 1.0, None, ALU.add))
                    own.settle()
                    dve.wait_ge(xT_in, 16)
                    for k in range(KC):
                        last = nc.vector.tensor_scalar(hT[:, k, :], xT[:, k, :], modc[:, KC + k:KC + k + 1], modc[:, k:k + 1],
                                                       ALU.mult, ALU.add)
                    last.then_inc(hT_ready, 1)
                elif kind == "modrow":
                    m = step[1]
                    key = ("ada", 4 + m)
                    w = chunk(dve, key)
                    if m >= 2:
                        b, n = PLACE[("modrow", m - 2)]
                        dve.wait_ge(bank_full[b], n + 1)
                    dve.wait_ge(cact_ready, 1)
                    part = acc[:, m % 2, :]
                    own.then(nc.vector.tensor_scalar(part, w[:, 0, :], cact[:, 0:1], None, ALU.mult))
                    for k in range(1, KC):
                        own.settle()
                        ins = nc.vector.scalar_tensor_tensor(part, w[:, k, :], cact[:, k:k + 1], part, ALU.mult, ALU.add)
                        if k < KC - 1:
                            own.then(ins)
                    ins.then_inc(acc_ready, 1)
                elif kind == "madd":
                    m = step[1]
                    dve.wait_ge(rows_in, 32)
                    src = filled(dve, ("modrow", m))
                    part = mod[:, m // 2, CH * (m % 2):CH * (m % 2) + CH]
                    one = 0.0 if m // 2 == SH2 else 1.0
                    nc.vector.scalar_tensor_tensor(part, src[:], one, part, ALU.add, ALU.add).then_inc(freed(("modrow", m)), 1)
                elif kind == "S":
                    u = step[1]
                    t, g, par, half = UNITS[u]
                    b0, n, j0 = unit_heads(u)
                    keys = P * (t + 1)
                    settle_bank(dve, ("tflip", j0 // 2))
                    settle_bank(dve, ("tflip", (j0 + n - 1) // 2))
                    src = filled(dve, step)
                    if u == 0:
                        dve.wait_ge(biasrow_out, 16)
                    if u >= 2:
                        b, m = PLACE[("Tr", u - 2)]
                        dve.wait_ge(bank_full[b], m + 1)
                    view = prob[:, u % 2, :].rearrange("p (j k) -> p j k", j=n)
                    nc.vector.scalar_tensor_tensor(view, src[:].rearrange("p (j k) -> p j k", j=n), SCALE,
                                                   toep[:, j0:j0 + n, P * (1 - t):T], ALU.mult, ALU.add).then_inc(freed(step), 1)
                    settle_bank(dve, step)
                    nc.vector.tensor_reduce(negmax[:, u, 0:n], view, AX.X, ALU.max, negate=True).then_inc(negmax_ready, 1)
                elif kind == "PV":
                    u = step[1]
                    t, g, par, half = UNITS[u]
                    b0, n, _ = unit_heads(u)
                    dve.wait_ge(exp_ready, u + 1)
                    own.then(nc.vector.reciprocal(prec[:, u, 0:n], psum_p[:, u, 0:n]))
                    own.settle()
                    src = filled(dve, step)
                    dst = y[:, t, :].rearrange("p (g b z c) -> p g b z c", g=2, z=2, c=HD)[:, g, b0:b0 + n, par, :]
                    nc.vector.tensor_tensor(dst, src[:, 0:HD * n].rearrange("p (j c) -> p j c", j=n),
                                            prec[:, u, 0:n].unsqueeze(2).broadcast_to([P, n, HD]), ALU.mult).then_inc(freed(step), 1)
                elif kind == "ny":
                    t = step[1]
                    dve.wait_ge(sq_ready, t + 1)
                    own.then(nc.vector.reciprocal(ystat[:, t, 2, :], ystat[:, t, 1, :]))
                    own.settle()
                    for g in range(2):
                        half = y[:, t, CH * g:CH * g + CH]
                        nc.vector.tensor_scalar(half, half, ystat[:, t, 2, g:g + 1], None, ALU.mult).then_inc(y_normed, 1)
                elif kind == "yT":
                    t, g = step[1:]
                    dve.wait_ge(gnsk_in, 32)
                    src = filled(dve, step)
                    nc.vector.tensor_tensor(yT[:, t, 4 * g:4 * g + 4, :], src[:].rearrange("p (j c) -> p j c", j=4),
                                            gn[:, 4 * g:4 * g + 4].unsqueeze(2).broadcast_to([P, 4, P]),
                                            ALU.mult).then_inc(freed(step), 1)
                elif kind == "ln1":
                    t = step[1]
                    dve.wait_ge(x_in, 16)
                    f = [(bank[PLACE[("wo", t, n)][0]][:], (bank_full[PLACE[("wo", t, n)][0]], PLACE[("wo", t, n)][1] + 1),
                          (bank_free[PLACE[("wo", t, n)][0]], PLACE[("wo", t, n)][1] + 1)) for n in range(2)]
                    normalise(t, mod[:, G1, :], f, x[:, t, :], x[:, t, :])
                    centre(t, x[:, t, :]).then_inc(normed_ready, 1)
                    dve.wait_ge(normed_ready, t + 1)
                    dve.wait_ge(rows2_ready, 1)
                    own.then(nc.vector.tensor_tensor(h2[:, t, :], x[:, t, :], mod[:, SC2, :], ALU.mult))
                    own.settle()
                    nc.vector.tensor_tensor(h2[:, t, :], h2[:, t, :], mod[:, SH2, :], ALU.add).then_inc(h2_ready, 1)
                    if t:
                        own.then(nc.vector.tensor_tensor(V_x1[:, t, :], x[:, t, :], lnw[:, 0, :], ALU.mult))
                        own.settle()
                        own.then(nc.vector.tensor_tensor(V_x1[:, t, :], V_x1[:, t, :], lnw[:, 1, :], ALU.add))
                elif kind == "route":
                    filled(dve, ("wo", 1, 1))
                    dve.sem_inc(slot_free, RING // 2)
                    filled(dve, ("s", 0, 0, 1))
                    for z in range(2):
                        settle_bank(dve, ("s", 0, 0, z))
                    before = own.n
                    for h in range(2):
                        route(0, scores[:, 0, h], h)
                    route_steps = (own.n - before) // 2

            dve.wait_ge(consts_in, 16)
            own.settle()
            for i in range(4):
                settle_bank(dve, ("s", i // 2, 1, i % 2))
                settle_bank(dve, ("s", 1, 0, i % 2))
            base = own.n

            def dots(turn, t, p0, p1):
                for p in range(p0, p1):
                    for s in (2 * p, 2 * p + 1):
                        r = (s + RING // 2) % RING
                        dve.wait_ge(slot_in[r], turn * (16 * PAIR // RING) + 16 * (s // RING + 1))
                        last = nc.vector.tensor_tensor_reduce(ring[:, r, 0:D], ring[:, r, 0:D], h2[:, t, :], 1.0, 0.0,
                                                              ALU.mult, ALU.add, pre[:, s:s + 1])
                    last.then_inc(dots_ready, 1)
                    dve.wait_ge(gelu_ready, turn * (PAIR // 2) + (p + 1))
                    for s in (2 * p, 2 * p + 1):
                        dve.wait_ge(slot_free, turn * PAIR + (RING + s - DIAGS + 1))
                        nc.vector.tensor_scalar(diag[:, s % DIAGS, :], ident, gel[:, s:s + 1],
                                                g_all[:, bass.ds(turn * PAIR + s, 1)], ALU.mult, ALU.mult).then_inc(diag_ready, 1)

            def turn_body(turn, t, routes):
                dots(turn, t, 0, 4)
                if routes:
                    route(turn + 1, scores_of(2 * turn + 2), 0)
                dots(turn, t, 4, 12)
                if routes:
                    route(turn + 1, scores_of(2 * turn + 3), 1)
                dots(turn, t, 12, 16)

            flat = H_s[:].rearrange("p (g z n) -> p g z n", z=2, n=NK)

            def scores_of(head):
                return flat[:, bass.ds(head, 1)].rearrange("p g z n -> p (g z) n")

            def ln2(t):
                f = [(fsum[:, n, :], (f_ready, t + 1), (f_taken, 2 * t + n + 1)) for n in range(2)]
                normalise(NT + t, mod[:, G2, :], f, V_x1[:, t, :], V_x1[:, t, :])
                own.then(centre(NT + t, V_x1[:, t, :]))
                own.settle()
                own.then(nc.vector.tensor_tensor(V_x1[:, t, :], V_x1[:, t, :], lnw[:, 2, :], ALU.mult))
                own.settle()
                nc.vector.tensor_tensor(V_x1[:, t, :], V_x1[:, t, :], lnw[:, 3, :], ALU.add).then_inc(out_ready, 1)

            with dve.Fori(0, TURNS) as turn:
                own.n = turn * (2 * route_steps) + base
                turn_body(turn, 0, True)
            own.n = base + TURNS * 2 * route_steps
            dve.wait_ge(x1_ready, 1)
            ln2(0)
            base = own.n - TURNS * 2 * route_steps
            with dve.Fori(TURNS, NT * TURNS - 1) as turn:
                own.n = turn * (2 * route_steps) + base
                turn_body(turn, 1, True)
            own.n = base + (NT * TURNS - 1) * 2 * route_steps
            turn_body(NT * TURNS - 1, 1, False)
            ln2(1)

        @block.gpsimd
        def _(pool):
            own = Steps(pool, pool_step)
            pool.wait_ge(rows_in, 32)
            for m in range(2, 6):
                settle_bank(pool, ("modrow", m))
            filled(pool, ("tflip", 7))
            own.then(nc.gpsimd.tensor_tensor(H_s[:, 0:D], lnw[:, 1, :], mod[:, SC2, :], ALU.mult))
            own.settle()
            own.then(nc.gpsimd.tensor_tensor(mod[:, SH2, :], mod[:, SH2, :], H_s[:, 0:D], ALU.add))
            own.then(nc.gpsimd.tensor_tensor(mod[:, SC2, :], mod[:, SC2, :], lnw[:, 0, :], ALU.mult))
            own.settle()
            pool.sem_inc(rows2_ready, 1)
            pool.wait_ge(normed_ready, 1)
            own.then(nc.gpsimd.tensor_tensor(V_x1[:, 0, :], x[:, 0, :], lnw[:, 0, :], ALU.mult))
            own.settle()
            nc.gpsimd.tensor_tensor(V_x1[:, 0, :], V_x1[:, 0, :], lnw[:, 1, :], ALU.add).then_inc(x1_ready, 1)

            with pool.Fori(0, NT * TURNS) as turn:
                for h in range(2):
                    pool.wait_ge(e_ready, turn * 2 + (h + 1))
                    pool.sem_inc(pool_gate, 1)
                    nc.gpsimd.tensor_copy(idx[:, h, :], e_all[:, bass.ds(turn * PAIR + TOPK * h, TOPK)]).then_inc(idx_staged, 1)
                    pool.wait_ge(idx_staged, turn * 2 + (h + 1))
                    pool.sem_inc(pool_gate, 1)
                    for k in range(TOPK):
                        s = TOPK * h + k
                        r = (s + RING // 2) % RING
                        pool.wait_ge(slot_free, turn * PAIR + (s + 1))
                        pool.sem_inc(pool_gate, 1)
                        nc.gpsimd.indirect_dma_start(ring[:, r, :], None, A["experts"],
                                                     bass.IndirectOffsetOnAxis(ap=idx[:, h, k:k + 1], axis=0)).then_inc(slot_in[r], 16)


def shape_constants():
    dist = (T - 1) - np.arange(ROW)
    n = np.maximum(dist, 1).astype(np.float32)
    large = BUCKETS // 2 + (np.log(n / 16) / math.log(2048 / 16) * 16).astype(np.int32)
    bucket = np.where(dist < 16, np.maximum(dist, 0), np.minimum(large, BUCKETS - 1))
    onehot = ((np.arange(BUCKETS)[:, None] == bucket) & (dist >= 0)).astype(np.float32)
    times = sum(((dist % d == 0) & (dist >= 0) & (dist <= w)).astype(np.int32) for w, d in ((128, 1), (512, 4), (2048, 16)))
    moba = np.where(dist >= 0, 0.0, MASKED)
    dil = np.where(times > 0, np.log(np.maximum(times, 1)), MASKED)
    maskrow = np.concatenate([np.tile(moba, (NH // 2, 1)), np.tile(dil, (NH // 2, 1))]).astype(np.float32)
    consts = np.concatenate([np.eye(P), np.eye(P)[::-1], np.tile(np.arange(TOPK), (P, 1))], 1).astype(np.float32)
    return onehot, maskrow, consts


def kernel(**inputs):
    import concourse.bacc as bacc
    from concourse.bass_utils import run_bass_kernel_spmd

    a = {k: np.asarray(v) for k, v in inputs.items()}

    def columns(v):
        return v.reshape(-1, P).T

    def chunks(w):
        return w.reshape(KC, P, -1, CH).transpose(2, 1, 0, 3).reshape(-1, P, KC * CH)

    w = {"ada": chunks(a["w_ada"][0]), "in": chunks(a["w_in"][0]), "out": chunks(a["w_out"][0]), "q": chunks(a["w_q_peer"][0])}
    order = [8 * g + 2 * b + par for g in range(2) for par in range(2) for b in range(4)]
    onehot, maskrow, consts = shape_constants()
    arrays = {
        "c": columns(a["c"][0]),
        "b_ada_c": columns(a["b_ada"][0, :2 * D]),
        "b_ada_r": a["b_ada"][:, 2 * D:],
        "w": np.stack([w[m][c] for m, c in STREAM]),
        "xT": a["x"][0].T.reshape(KC, P, T).transpose(1, 0, 2).reshape(P, KC * T),
        "x": a["x"][0],
        "ln": np.concatenate([a["ln1_g"], a["ln1_b"], a["ln2_g"], a["ln2_b"]], 1),
        "gn": columns(np.concatenate([a["gn_moba"][0], a["gn_dil"][0]])),
        "skT": a["sub_keys"][0].transpose(0, 2, 1).reshape(P, NK),
        "relT": a["rel_bias"][order].T,
        "experts": np.concatenate([a["peer_u"][0], a["peer_v"][0]], 1),
        "onehot": onehot, "maskrow": maskrow, "consts": consts,
    }
    nc = bacc.Bacc("TRN2", target_bir_lowering=False, num_devices=1)
    feeds, A = {}, {}
    for name, v in arrays.items():
        v = np.ascontiguousarray(v)
        feeds[f"in_{name}"] = v
        A[name] = nc.dram_tensor(f"in_{name}", v.shape, mybir.dt.from_np(v.dtype), kind="ExternalInput").ap()
    A["scratch"] = nc.dram_tensor("scratch", (NH, ROW), F32, kind="Internal").ap()
    out = nc.dram_tensor("out_x", (1, T, D), F32, kind="ExternalOutput").ap()
    build(nc, A, out)
    r = run_bass_kernel_spmd(nc, [feeds], core_ids=[0])
    return r.results[0]["out_x"]
```

```python
import math
from contextlib import ExitStack

import numpy as np
import concourse.bass as bass
from concourse import mybir

F32 = mybir.dt.float32
I32 = mybir.dt.int32
U32 = mybir.dt.uint32
ALU = mybir.AluOpType
ACT = mybir.ActivationFunctionType
AX = mybir.AxisListType

P = 128
D = 1024
T = 256
NT = T // P
KC = D // P
HD = 64
NH = 16
CH = 512
BUCKETS = 32
ROW = 384
MASKED = -1e30
ALPHA = 2.0 ** 0.25
EPS = 1e-5
SCALE = HD ** -0.5
PH = 8
NK = 128
TOPK = 16
SLOTS = PH * TOPK
PAIR = 2 * TOPK
TURNS = SLOTS // PAIR
RING = 8
WRING = 4
TAKEN = -3e38
DIAGS = 4

STREAM = [("ada", 0), ("ada", 1), ("ada", 2), ("ada", 3), ("in", 0), ("in", 1), ("ada", 4), ("ada", 5), ("in", 2),
          ("ada", 6), ("in", 3), ("ada", 7), ("in", 4), ("ada", 8), ("ada", 9), ("in", 5), ("ada", 10), ("ada", 11),
          ("out", 0), ("out", 1), ("q", 0), ("q", 1)]
G1, SH2, SC2, G2 = range(4)
UNITS = [(0, 0, 0, 0), (0, 0, 1, 0), (1, 0, 0, 0), (0, 1, 0, 0), (0, 1, 1, 0), (1, 0, 0, 1), (1, 0, 1, 0), (1, 0, 1, 1),
         (1, 1, 0, 0), (1, 1, 0, 1), (1, 1, 1, 0), (1, 1, 1, 1)]
PLAN = (
    [("bias",)] + [("wsum", c) for c in range(4)] + [("modc",), ("qk", 0, 0), ("qk", 0, 1), ("qk", 1, 0), ("qk", 1, 1)]
    + [("wsum", 4), ("wsum", 5)] + [("tflip", j) for j in range(4)]
    + [("modrow", 0), ("modrow", 1), ("S", 0), ("S", 1), ("v", 0, 0), ("wsum", 6), ("Tr", 0), ("Tr", 1), ("modrow", 2),
       ("v", 0, 1), ("PV", 0), ("PV", 1), ("S", 2), ("qk", 2, 0), ("wsum", 7), ("Tr", 2), ("modrow", 3), ("qk", 2, 1),
       ("PV", 2), ("qk", 3, 0), ("wsum", 8), ("modrow", 4), ("qk", 3, 1), ("wsum", 9)]
    + [("tflip", j) for j in range(4, 8)]
    + [("modrow", 5), ("S", 3), ("S", 4), ("v", 1, 0), ("wsum", 10), ("Tr", 3), ("Tr", 4), ("S", 5), ("PV", 3), ("PV", 4),
       ("v", 1, 1), ("modrow", 6), ("ny", 0), ("Tr", 5), ("S", 6), ("yT", 0, 0), ("yT", 0, 1), ("PV", 5), ("Tr", 6), ("S", 7),
       ("wo", 0, 0), ("PV", 6), ("Tr", 7), ("S", 8), ("wsum", 11), ("wo", 0, 1), ("modrow", 7), ("PV", 7), ("ln1a", 0),
       ("Tr", 8), ("S", 9), ("PV", 8), ("rows2",), ("ln1b", 0), ("Tr", 9), ("S", 10), ("PV", 9), ("hT", 0, 0), ("hT", 0, 1),
       ("Tr", 10), ("S", 11), ("q", 0, 0), ("PV", 10), ("Tr", 11), ("s", 0, 0, 0), ("s", 0, 0, 1), ("PV", 11), ("q", 0, 1),
       ("free", 0), ("ny", 1), ("yT", 1, 0), ("yT", 1, 1), ("route", 0), ("wo", 1, 0), ("free", 1), ("wo", 1, 1), ("free", 2),
       ("ln1a", 1), ("q", 0, 2), ("q", 0, 3), ("s", 0, 1, 0), ("s", 0, 1, 1), ("s", 0, 2, 0), ("s", 0, 2, 1), ("s", 0, 3, 0),
       ("s", 0, 3, 1), ("ln1b", 1), ("hT", 1, 0), ("hT", 1, 1), ("dots", 0), ("dots", 1), ("q", 1, 2), ("slots", 0),
       ("slots", 1), ("dots", 2), ("slots", 2), ("dots", 3), ("slots", 3), ("q", 1, 3), ("route", 1), ("q", 1, 0),
       ("q", 1, 1), ("dots", 4), ("slots", 4), ("dots", 5), ("slots", 5)] + [("s", 1, i, z) for i in range(4) for z in range(2)]
    + [(kind, p) for p in range(6, 9) for kind in ("dots", "slots")] + [("route", 2)]
    + [(kind, p) for p in range(9, 13) for kind in ("dots", "slots")] + [("route", 3)]
    + [(kind, p) for p in range(13, 16) for kind in ("dots", "slots")]
)
for _m in range(8):
    PLAN.insert(PLAN.index(("modrow", _m)) + 3, ("madd", _m))
CHUNK = {key: n for n, key in enumerate(STREAM)}
STEP_BANKS = 6
NO_FILL = ("ny", "ln1a", "ln1b", "route", "rows2", "madd", "wsum", "free", "dots", "slots")
FILLS = [s for s in PLAN if s[0] not in NO_FILL]
LATE = [("wo", t, n) for t in range(NT) for n in range(2)]
PLACE = {s: (n % STEP_BANKS, n // STEP_BANKS) for n, s in enumerate(s for s in FILLS if s not in LATE)}
PLACE |= {s: (STEP_BANKS + n % 2, n // 2) for n, s in enumerate(LATE)}


def unit_heads(u):
    t, g, par, half = UNITS[u]
    b0, n = (0, 4) if t == 0 else (2 * half, 2)
    return b0, n, 8 * g + 4 * par + b0


class Steps:

    def __init__(self, eng, sem):
        self.eng, self.sem, self.n = eng, sem, 0

    def then(self, ins):
        ins.then_inc(self.sem, 1)
        self.n = self.n + 1

    def settle(self):
        self.eng.wait_ge(self.sem, self.n)

    def settle_here(self, gate):
        self.settle()
        self.eng.sem_inc(gate, 1)


def build(nc, A, out):
    ctx = ExitStack()
    with ctx:
        def sb(name, shape, dt=F32):
            return ctx.enter_context(nc.sbuf_tensor(name, shape, dt))

        def sem(name):
            return ctx.enter_context(nc.semaphore(name))

        ring = sb("ring", [P, RING, 2 * D])
        wring = ring[:].rearrange("p r c -> p (r c)").rearrange("p (w k n) -> p w k n", w=WRING, k=KC)
        xT_y = sb("xT_y", [P, KC * T])
        xT = xT_y[:].rearrange("p (k t) -> p k t", k=KC)
        y = xT_y[:].rearrange("p (t c) -> p t c", t=NT)
        hT_yT = sb("hT_yT", [P, KC * T])
        hT = hT_yT[:].rearrange("p (k t) -> p k t", k=KC)
        yT = hT_yT[:].rearrange("p (t k c) -> p t k c", t=NT, k=KC)
        x = sb("x", [P, NT, D])
        QT_h2T = sb("QT_h2T", [P, KC * T])
        QT = QT_h2T[:].rearrange("p (b t) -> p b t", b=KC)
        h2T = QT_h2T[:].rearrange("p (t k c) -> p t k c", t=NT, k=KC)
        KT_qT = sb("KT_qT", [P, KC * T])
        KT = KT_qT[:].rearrange("p (b t) -> p b t", b=KC)
        qT = KT_qT[:].rearrange("p (t h c) -> p t h c", t=NT, h=PH)
        V_x1 = sb("V_x1", [P, NT, D])
        H_s = sb("H_s", [P, NH * T])
        hankel = H_s[:].rearrange("p (h k) -> p h k", h=NH)
        scores = H_s[:].rearrange("p (t h z n) -> p t h z n", t=NT, h=PH, z=2)
        T_h2 = sb("T_h2", [P, NH * T])
        toep = T_h2[:].rearrange("p (h k) -> p h k", h=NH)
        h2 = T_h2[:, 0:NT * D].rearrange("p (t c) -> p t c", t=NT)
        mod = sb("mod", [P, 4, D])
        lnw = sb("lnw", [P, 4, D])
        halves = {"high": (T_h2[:, NT * D:], xT_y[:]), "low": (None, hT_yT[:])}
        acc = sb("acc", [P, 4, CH])
        probs = sb("probs", [P, 4 * CH])
        prob = probs[:, 0:2 * CH].rearrange("p (u k) -> p u k", u=2)
        probT = probs[:, 2 * CH:].rearrange("p (u k) -> p u k", u=2)
        halves["low"] = (probs[:], hT_yT[:])
        onehot = probT[0:BUCKETS, 0, 0:ROW]
        maskrow = probT[0:NH, 1, 0:ROW]
        biasrow = prob[0:NH, 0, 0:ROW]
        relT = sb("relT", [BUCKETS, NH])
        consts = sb("consts", [P, 2 * P + TOPK])
        ident, flip, iota = consts[:, 0:P], consts[:, P:2 * P], consts[:, 2 * P:2 * P + TOPK]
        ones = sb("ones", [P, P])
        zeros = sb("zeros", [P, P])
        cin = sb("cin", [P, KC])
        ctanh = sb("ctanh", [P, KC])
        cact = sb("cact", [P, KC])
        badac = sb("badac", [P, 2 * KC])
        modc = sb("modc", [P, 2 * KC])
        gn = sb("gn", [P, KC])
        skT = sb("skT", [P, NK])
        epsc = sb("epsc", [P, 1])
        spare = sb("spare", [P, 1])
        negmax = sb("negmax", [P, len(UNITS), 4])
        psum_p = sb("psum_p", [P, len(UNITS), 4])
        prec = sb("prec", [P, len(UNITS), 4])
        ystat = sb("ystat", [P, NT, 3, 2])
        lnst = sb("lnst", [P, 2 * NT, 6])
        junk = sb("junk", [P, D], mybir.dt.bfloat16)
        diag = sb("diag", [P, DIAGS, P])
        swork = sb("swork", [P, 2, 2, NK])
        v16 = sb("v16", [P, 2, TOPK])
        i16 = sb("i16", [P, 2, TOPK], U32)
        cand = acc[:, 2, :].rearrange("p (i n) -> p i n", i=2)
        best = sb("best", [P, TOPK])
        pos = sb("pos", [P, TOPK], U32)
        pij = sb("pij", [P, 2, TOPK], U32)
        eq = acc[:, 3, :].rearrange("p (z k n) -> p z k n", z=2, k=TOPK)
        eij = sb("eij", [P, 2, TOPK])
        esum = sb("esum", [P, TOPK])
        bdiff = sb("bdiff", [P, TOPK])
        bexp = sb("bexp", [P, TOPK])
        bsum = sb("bsum", [P, 2])
        e_all = sb("e_all", [P, NT * SLOTS], I32)
        g_all = sb("g_all", [P, NT * SLOTS])
        pre = sb("pre", [P, PAIR])
        gel = sb("gel", [P, PAIR])
        idx = sb("idx", [P, 2, TOPK], I32)
        bank = [ctx.enter_context(nc.psum_tensor(f"bank{i}", [P, CH], F32))[:] for i in range(STEP_BANKS)]
        fsum = ctx.enter_context(nc.psum_tensor("fsum", [P, 2, CH], F32))
        bank += [fsum[:, 0, :], fsum[:, 1, :]]

        bank_full = [sem(f"bank_full{i}") for i in range(len(bank))]
        bank_free = [sem(f"bank_free{i}") for i in range(len(bank))]
        w_in = [sem(f"w_in{i}") for i in range(WRING)]
        c_in, bias_in, xT_in, consts_in, x_in, rows_in, ln_in, gnsk_in = (sem(n) for n in (
            "c_in", "bias_in", "xT_in", "consts_in", "x_in", "rows_in", "ln_in", "gnsk_in"))
        wq_in = {"high": sem("wq_high_in"), "low": sem("wq_low_in")}
        biasrow_out, hankel_in = sem("biasrow_out"), sem("hankel_in")
        tanh_ready, cact_ready, hT_ready = sem("tanh_ready"), sem("cact_ready"), sem("hT_ready")
        acc_ready = sem("acc_ready")
        negmax_ready, exp_ready = sem("negmax_ready"), sem("exp_ready")
        sq_ready, y_normed = sem("sq_ready"), sem("y_normed")
        mean_ready, std_ready = sem("mean_ready"), sem("std_ready")
        normed_ready, x1_ready, h2_ready, rows2_ready = sem("normed_ready"), sem("x1_ready"), sem("h2_ready"), sem("rows2_ready")
        set_ready = sem("set_ready")
        dve_step, act_step, pool_step = sem("dve_step"), sem("act_step"), sem("pool_step")
        dve_gate, pool_gate = sem("dve_gate"), sem("pool_gate")
        best_ready, bexp_ready, e_ready = sem("best_ready"), sem("bexp_ready"), sem("e_ready")
        idx_staged = sem("idx_staged")
        slot_in = [sem(f"slot_in{i}") for i in range(RING)]
        slot_free = sem("slot_free")
        dots_ready, gelu_ready, diag_ready = sem("dots_ready"), sem("gelu_ready"), sem("diag_ready")
        f_ready, f_taken, out_ready, out_done = sem("f_ready"), sem("f_taken"), sem("out_ready"), sem("out_done")

        def filled(eng, step):
            b, n = PLACE[step]
            eng.wait_ge(bank_full[b], n + 1)
            return bank[b]

        def freed(step):
            return bank_free[PLACE[step][0]]

        def settle_bank(eng, step):
            b, n = PLACE[step]
            eng.wait_ge(bank_free[b], n + 1)

        def chunk(eng, key):
            n = CHUNK[key]
            eng.wait_ge(w_in[n % WRING], 16 * (n // WRING + 1))
            return wring[:, n % WRING]

        def query_weights(eng, t, i):
            if t == 0 and i < 2:
                return lambda k, w=chunk(eng, ("q", 0)): w[:, k, :]
            part = "low" if i < 2 else "high"
            eng.wait_ge(wq_in[part], 32)
            w = [half.rearrange("p (k n) -> p k n", n=CH) for half in halves[part]]
            return lambda k: w[k // (KC // 2)][:, k % (KC // 2), :]

        def chunk_used(eng, key):
            m, c = key
            if m == "ada":
                eng.wait_ge(acc_ready, c + 1)
            elif m == "in":
                filled(eng, (("qk", 0, 1), ("qk", 1, 1), ("v", 0, 1), ("qk", 2, 1), ("qk", 3, 1), ("v", 1, 1))[c])
            else:
                raise ValueError("nothing follows this chunk")

        block = ctx.enter_context(nc.Block())

        @block.sync
        def _(sp):
            sp.dma_start(cin[:], A["c"]).then_inc(c_in, 16)
            sp.dma_start(badac[:], A["b_ada_c"]).then_inc(c_in, 16)
            for name, dst in (("relT", relT[:]), ("onehot", onehot), ("maskrow", maskrow)):
                sp.dma_start(dst, A[name]).then_inc(bias_in, 16)
            sp.dma_start(consts[:], A["consts"]).then_inc(consts_in, 16)

            def load(n):
                if n >= WRING:
                    chunk_used(sp, STREAM[n - WRING])
                sp.dma_start(wring[:, n % WRING], A["w"][n].rearrange("p (k n) -> p k n", k=KC)).then_inc(w_in[n % WRING], 16)

            load(0)
            load(1)
            load(2)
            load(3)
            sp.dma_start(xT, A["xT"].rearrange("p (k t) -> p k t", k=KC)).then_inc(xT_in, 16)
            load(4)
            load(5)
            settle_bank(sp, ("bias",))
            sp.dma_start(A["scratch"], biasrow).then_inc(biasrow_out, 16)
            sp.wait_ge(biasrow_out, 16)
            shifts = bass.AP(A["scratch"].tensor, 0, [[1, P], [ROW, NH], [1, T]])
            sp.dma_start(hankel, shifts).then_inc(hankel_in, 16)
            for n in range(WRING + 2, len(STREAM) - 1):
                load(n)
                if n == 7:
                    sp.dma_start(mod[:].rearrange("p r c -> p (r c)"), A["b_ada_r"].broadcast_to([P, 4 * D])).then_inc(rows_in, 16)
                if n == 8:
                    sp.dma_start(x[:], A["x"].rearrange("(t p) c -> p t c", p=P)).then_inc(x_in, 16)
                    sp.dma_start(gn[:], A["gn"]).then_inc(gnsk_in, 16)
                    sp.dma_start(skT[:], A["skT"]).then_inc(gnsk_in, 16)
                if n == 13:
                    sp.dma_start(lnw[:].rearrange("p r c -> p (r c)"), A["ln"].broadcast_to([P, 4 * D])).then_inc(ln_in, 16)

            def load_half(part, z):
                n = CHUNK[("q", 1 if part == "high" else 0)]
                sp.dma_start(halves[part][z], A["w"][n, :, 2 * D * z:2 * D * z + 2 * D]).then_inc(wq_in[part], 16)

            settle_bank(sp, ("S", len(UNITS) - 1))
            load_half("high", 0)
            filled(sp, ("yT", 1, 0))
            filled(sp, ("yT", 1, 1))
            load_half("high", 1)
            filled(sp, ("PV", len(UNITS) - 1))
            load_half("low", 0)
            filled(sp, ("wo", 1, 1))
            load_half("low", 1)
            for t in range(NT):
                sp.wait_ge(out_ready, t + 1)
                sp.dma_start(out[0, P * t:P * t + P, :], V_x1[:, t, :]).then_inc(out_done, 16)
            sp.wait_ge(out_done, 16 * NT)

        @block.tensor
        def _(pe):
            def open_bank(step):
                b, n = PLACE[step]
                if n:
                    pe.wait_ge(bank_free[b], n)
                return bank[b], bank_full[b]

            def product(dst, lhs, rhs, n=KC):
                for k in range(n):
                    last = nc.tensor.matmul(dst, lhs(k), rhs(k), start=(k == 0), stop=(k == n - 1))
                return last

            def slot(turn, s, opens=False):
                if opens:
                    for step in LATE[-2:]:
                        settle_bank(pe, step)
                pe.wait_ge(diag_ready, turn * PAIR + (s + 1))
                for n in range(2):
                    last = nc.tensor.matmul(fsum[:, n, :], diag[:, s % DIAGS, :],
                                            ring[:, s % RING, D + CH * n:D + CH * n + CH], start=opens, stop=False)
                last.then_inc(slot_free, 1)

            for step in PLAN:
                kind = step[0]
                if kind == "slots":
                    for s in (2 * step[1], 2 * step[1] + 1):
                        slot(0, s, opens=(s == 0))
                if kind in NO_FILL:
                    continue
                dst, full = open_bank(step)
                if kind == "bias":
                    pe.wait_ge(bias_in, 48)
                    nc.tensor.matmul(dst[0:NH, 0:ROW], relT[:], onehot, start=True, stop=True).then_inc(full, 1)
                elif kind == "modc":
                    pe.wait_ge(set_ready, 1)
                    for c in range(4):
                        pe.wait_ge(acc_ready, c + 1)
                        for j in range(4):
                            last = nc.tensor.matmul(dst[:, 4 * c + j:4 * c + j + 1], acc[:, c, P * j:P * j + P],
                                                    ones[:, 0:1], start=True, stop=True)
                    last.then_inc(full, 1)
                elif kind == "qk":
                    c, i = step[1:]
                    key = ("in", (0, 1, 3, 4)[c])
                    w = chunk(pe, key)
                    pe.wait_ge(hT_ready, 1)
                    for j in range(2):
                        last = product(dst[:, T * j:T * j + T], lambda k: w[:, k, P * (2 * i + j):P * (2 * i + j) + P],
                                       lambda k: hT[:, k, :])
                    last.then_inc(full, 1)
                elif kind == "v":
                    g, t = step[1:]
                    w = chunk(pe, ("in", 2 + 3 * g))
                    product(dst[:], lambda k: hT[:, k, P * t:P * t + P], lambda k: w[:, k, :]).then_inc(full, 1)
                elif kind == "tflip":
                    pe.wait_ge(consts_in, 16)
                    pe.wait_ge(hankel_in, 16)
                    nc.tensor.matmul(dst[:], flip, H_s[:, CH * step[1]:CH * step[1] + CH], start=True, stop=True).then_inc(full, 1)
                elif kind == "modrow":
                    pe.wait_ge(set_ready, 1)
                    pe.wait_ge(acc_ready, step[1] + 5)
                    nc.tensor.matmul(dst[:], ones[:], acc[:, step[1] % 4, :], start=True, stop=True).then_inc(full, 1)
                elif kind == "S":
                    t, g, par, half = UNITS[step[1]]
                    b0, n, _ = unit_heads(step[1])
                    for i in range(2):
                        settle_bank(pe, ("qk", 2 * g, i))
                        settle_bank(pe, ("qk", 2 * g + 1, i))
                    r = slice(HD * par, HD * par + HD)
                    keys = P * (t + 1)
                    for j in range(n):
                        last = nc.tensor.matmul(dst[:, keys * j:keys * j + keys], QT[r, 4 * g + b0 + j, P * t:P * t + P],
                                                KT[r, 4 * g + b0 + j, 0:keys], start=True, stop=True)
                    last.then_inc(full, 1)
                elif kind == "Tr":
                    pe.wait_ge(exp_ready, step[1] + 1)
                    pe.wait_ge(consts_in, 16)
                    for j in range(4):
                        last = nc.tensor.transpose(dst[:, P * j:P * j + P], prob[:, step[1] % 2, P * j:P * j + P], ident)
                    last.then_inc(full, 1)
                elif kind == "PV":
                    t, g, par, half = UNITS[step[1]]
                    b0, n, _ = unit_heads(step[1])
                    settle_bank(pe, ("Tr", step[1]))
                    for tt in range(t + 1):
                        settle_bank(pe, ("v", g, tt))
                    for j in range(n):
                        c = D // 2 * g + P * (b0 + j) + HD * par
                        for kt in range(t + 1):
                            at = P * ((t + 1) * j + kt)
                            last = nc.tensor.matmul(dst[:, HD * j:HD * j + HD], probT[:, step[1] % 2, at:at + P],
                                                    V_x1[:, kt, c:c + HD], start=(kt == 0), stop=(kt == t))
                    last.then_inc(full, 1)
                elif kind == "yT":
                    t, g = step[1:]
                    pe.wait_ge(y_normed, 2 * t + 2)
                    for j in range(4):
                        last = nc.tensor.transpose(dst[:, P * j:P * j + P], y[:, t, P * (4 * g + j):P * (4 * g + j) + P], ident)
                    last.then_inc(full, 1)
                elif kind == "wo":
                    t, n = step[1:]
                    w = chunk(pe, ("out", n))
                    settle_bank(pe, ("yT", t, 0))
                    settle_bank(pe, ("yT", t, 1))
                    product(dst[:], lambda k: yT[:, t, k, :], lambda k: w[:, k, :]).then_inc(full, 1)
                elif kind == "hT":
                    t, i = step[1:]
                    pe.wait_ge(h2_ready, t + 1)
                    for j in range(4):
                        last = nc.tensor.transpose(dst[:, P * j:P * j + P], h2[:, t, P * (4 * i + j):P * (4 * i + j) + P], ident)
                    last.then_inc(full, 1)
                elif kind == "q":
                    t, i = step[1:]
                    w = query_weights(pe, t, i)
                    settle_bank(pe, ("hT", t, 0))
                    settle_bank(pe, ("hT", t, 1))
                    for j in range(2):
                        c = P * (2 * (i % 2) + j)
                        last = product(dst[:, P * j:P * j + P], lambda k: w(k)[:, c:c + P], lambda k: h2T[:, t, k, :])
                    last.then_inc(full, 1)
                elif kind == "s":
                    t, i, z = step[1:]
                    pe.wait_ge(gnsk_in, 32)
                    settle_bank(pe, ("q", t, i))
                    r = slice(HD * z, HD * z + HD)
                    for j in range(2):
                        last = nc.tensor.matmul(dst[:, P * j:P * j + P], qT[r, t, 2 * i + j, :], skT[r, :], start=True, stop=True)
                    last.then_inc(full, 1)

            for t in range(NT):
                if t:
                    pe.wait_ge(f_taken, 2 * t)
                    for n in range(2):
                        nc.tensor.matmul(fsum[:, n, :], zeros[:], prob[:, 0, :], start=True, stop=False)
                with pe.Fori(TURNS * t if t else 1, TURNS * (t + 1)) as turn:
                    for s in range(PAIR):
                        slot(turn, s)
                for n in range(2):
                    last = nc.tensor.matmul(fsum[:, n, 0:1], zeros[:], prob[:, 0, 0:1], start=False, stop=True)
                last.then_inc(f_ready, 1)

        @block.scalar
        def _(act):
            own = Steps(act, act_step)
            act.wait_ge(set_ready, 1)
            act.wait_ge(c_in, 32)
            nc.scalar.activation(ctanh[:], cin[:], ACT.Tanh, scale=0.5).then_inc(tanh_ready, 1)

            def route_exp(head):
                act.wait_ge(best_ready, head + 1)
                nc.scalar.activation(bexp[:], bdiff[:], ACT.Exp, accum_out=bsum[:, 0:1]).then_inc(bexp_ready, 1)

            def gelus(turn, p0, p1):
                for p in range(p0, p1):
                    act.wait_ge(dots_ready, turn * (PAIR // 2) + (p + 1))
                    nc.scalar.activation(gel[:, 2 * p:2 * p + 2], pre[:, 2 * p:2 * p + 2], ACT.Gelu).then_inc(gelu_ready, 1)

            def load_sqrt():
                own.settle()
                own.then(nc.scalar.activation(spare[:], epsc[:], ACT.Sqrt))

            def evacuate(step, dst, src):
                nc.scalar.copy(dst, src).then_inc(freed(step), 1)

            def deviation(i, z):
                load_sqrt()
                act.wait_ge(mean_ready, i + 1)
                own.settle()
                own.then(nc.scalar.activation(junk[:], z, ACT.Square, bias=lnst[:, i, 2:3], accum_out=lnst[:, i, 3:4]))
                own.settle()
                nc.scalar.activation(lnst[:, i, 4:5], lnst[:, i, 3:4], ACT.Sqrt, bias=epsc[:], scale=1.0 / D).then_inc(std_ready, 1)

            for step in PLAN:
                kind = step[0]
                if kind == "tflip":
                    src = filled(act, step)
                    evacuate(step, T_h2[:, CH * step[1]:CH * step[1] + CH], src[:])
                elif kind == "qk":
                    c, i = step[1:]
                    dst = (QT, KT)[c % 2][:, 4 * (c // 2) + 2 * i:4 * (c // 2) + 2 * i + 2, :]
                    evacuate(step, dst, filled(act, step)[:].rearrange("p (j t) -> p j t", j=2))
                elif kind == "v":
                    g, t = step[1:]
                    evacuate(step, V_x1[:, t, CH * g:CH * g + CH], filled(act, step)[:])
                elif kind == "S":
                    t = UNITS[step[1]][0]
                    _, n, _ = unit_heads(step[1])
                    keys = P * (t + 1)
                    act.wait_ge(negmax_ready, step[1] + 1)
                    for j in range(n):
                        part = prob[:, step[1] % 2, keys * j:keys * j + keys]
                        last = nc.scalar.activation(part, part, ACT.Exp, bias=negmax[:, step[1], j:j + 1],
                                                    accum_out=psum_p[:, step[1], j:j + 1])
                    last.then_inc(exp_ready, 1)
                elif kind == "Tr":
                    if step[1] >= 2:
                        b, n = PLACE[("PV", step[1] - 2)]
                        act.wait_ge(bank_full[b], n + 1)
                    evacuate(step, probT[:, step[1] % 2, :], filled(act, step)[:])
                elif kind == "ny":
                    t = step[1]
                    load_sqrt()
                    for u, unit in enumerate(UNITS):
                        if unit[0] == t:
                            settle_bank(act, ("PV", u))
                    for g in range(2):
                        own.then(nc.scalar.activation(junk[:, 0:CH], y[:, t, CH * g:CH * g + CH], ACT.Square,
                                                      accum_out=ystat[:, t, 0, g:g + 1]))
                        own.settle()
                    nc.scalar.activation(ystat[:, t, 1, :], ystat[:, t, 0, :], ACT.Sqrt, bias=epsc[:],
                                         scale=1.0 / CH).then_inc(sq_ready, 1)
                elif kind == "ln1a":
                    t = step[1]
                    deviation(t, x[:, t, :])
                elif kind == "hT":
                    t, i = step[1:]
                    evacuate(step, h2T[:, t, 4 * i:4 * i + 4, :], filled(act, step)[:].rearrange("p (j c) -> p j c", j=4))
                elif kind == "q":
                    t, i = step[1:]
                    evacuate(step, qT[:, t, 2 * i:2 * i + 2, :], filled(act, step)[:, 0:2 * P].rearrange("p (j c) -> p j c", j=2))
                elif kind == "s":
                    t, i, z = step[1:]
                    evacuate(step, scores[:, t, 2 * i:2 * i + 2, z, :], filled(act, step)[:, 0:2 * P].rearrange("p (j n) -> p j n", j=2))
                elif kind == "route":
                    route_exp(step[1])
                elif kind == "free":
                    if step[1] == 0:
                        act.wait_ge(acc_ready, 12)
                        filled(act, ("q", 0, 1))
                        act.sem_inc(slot_free, RING // 2)
                    else:
                        filled(act, ("wo", 1, step[1] - 1))
                        act.sem_inc(slot_free, RING // 4)
                elif kind == "dots":
                    gelus(0, step[1], step[1] + 1)

            def turn_body(turn, routes):
                gelus(turn, 0, 2)
                if routes:
                    route_exp(2 * turn + 2)
                gelus(turn, 2, 8)
                if routes:
                    route_exp(2 * turn + 3)
                gelus(turn, 8, 16)

            with act.Fori(1, TURNS) as turn:
                turn_body(turn, True)
            deviation(NT, V_x1[:, 0, :])
            with act.Fori(TURNS, NT * TURNS - 1) as turn:
                turn_body(turn, True)
            turn_body(NT * TURNS - 1, False)
            deviation(NT + 1, V_x1[:, 1, :])

        @block.vector
        def _(dve):
            own = Steps(dve, dve_step)
            nc.vector.memset(ones[:], 1.0)
            nc.vector.memset(zeros[:], 0.0)
            nc.vector.memset(epsc[:], EPS).then_inc(set_ready, 1)

            def normalise(i, gate, f, res, z):
                for n in range(2):
                    src, ready, taken = f[n]
                    own.settle()
                    dve.wait_ge(*ready)
                    nc.vector.tensor_tensor(acc[:, n, :], src, gate[:, CH * n:CH * n + CH], ALU.mult).then_inc(taken[0], 1)
                    dve.wait_ge(*taken)
                    own.then(nc.vector.scalar_tensor_tensor(z[:, CH * n:CH * n + CH], res[:, CH * n:CH * n + CH], ALPHA,
                                                            acc[:, n, :], ALU.mult, ALU.add, accum_out=lnst[:, i, n:n + 1]))
                own.settle()
                nc.vector.tensor_scalar(lnst[:, i, 2:3], lnst[:, i, 0:1], lnst[:, i, 1:2], -1.0 / D,
                                        ALU.add, ALU.mult).then_inc(mean_ready, 1)

            def centre(i, z):
                dve.wait_ge(std_ready, i + 1)
                own.then(nc.vector.reciprocal(lnst[:, i, 5:6], lnst[:, i, 4:5]))
                own.settle()
                return nc.vector.tensor_scalar(z, z, lnst[:, i, 2:3], lnst[:, i, 5:6], ALU.add, ALU.mult)

            def dots(turn, t, p0, p1):
                for p in range(p0, p1):
                    for s in (2 * p, 2 * p + 1):
                        r = s % RING
                        dve.wait_ge(slot_in[r], turn * (16 * PAIR // RING) + 16 * (s // RING + 1))
                        last = nc.vector.tensor_tensor_reduce(ring[:, r, 0:D], ring[:, r, 0:D], h2[:, t, :], 1.0, 0.0,
                                                              ALU.mult, ALU.add, pre[:, s:s + 1])
                    last.then_inc(dots_ready, 1)
                    dve.wait_ge(gelu_ready, turn * (PAIR // 2) + (p + 1))
                    for s in (2 * p, 2 * p + 1):
                        dve.wait_ge(slot_free, turn * PAIR + (RING + s - DIAGS + 1))
                        nc.vector.tensor_scalar(diag[:, s % DIAGS, :], ident, gel[:, s:s + 1],
                                                g_all[:, bass.ds(turn * PAIR + s, 1)], ALU.mult, ALU.mult).then_inc(diag_ready, 1)

            def route(turn, both, h):
                def settle():
                    own.settle_here(dve_gate)

                settle()
                own.then(nc.vector.tensor_copy(swork[:, 0], both))
                settle()
                for z in range(2):
                    own.then(nc.vector.max(v16[:, z, 0:8], swork[:, 0, z, :]))
                settle()
                for z in range(2):
                    own.then(nc.vector.max_index(i16[:, z, 0:8], v16[:, z, 0:8], swork[:, 0, z, :]))
                    own.then(nc.vector.match_replace(swork[:, 1, z, :], v16[:, z, 0:8], swork[:, 0, z, :], TAKEN))
                settle()
                for z in range(2):
                    own.then(nc.vector.max(v16[:, z, 8:16], swork[:, 1, z, :]))
                settle()
                for z in range(2):
                    own.then(nc.vector.max_index(i16[:, z, 8:16], v16[:, z, 8:16], swork[:, 1, z, :]))
                square = [P, TOPK, TOPK]
                own.then(nc.vector.tensor_tensor(cand[:, 0, :].rearrange("p (i j) -> p i j", i=TOPK),
                                                 v16[:, 0, :].unsqueeze(2).broadcast_to(square),
                                                 v16[:, 1, :].unsqueeze(1).broadcast_to(square), ALU.add))
                settle()
                own.then(nc.vector.max(best[:, 0:8], cand[:, 0, :]))
                settle()
                own.then(nc.vector.max_index(pos[:, 0:8], best[:, 0:8], cand[:, 0, :]))
                own.then(nc.vector.match_replace(cand[:, 1, :], best[:, 0:8], cand[:, 0, :], TAKEN))
                settle()
                own.then(nc.vector.max(best[:, 8:16], cand[:, 1, :]))
                settle()
                nc.vector.tensor_scalar(bdiff[:], best[:], best[:, 0:1], None, ALU.subtract).then_inc(best_ready, 1)
                own.then(nc.vector.max_index(pos[:, 8:16], best[:, 8:16], cand[:, 1, :]))
                settle()
                own.then(nc.vector.tensor_scalar(pij[:, 0, :], pos[:], 4, None, ALU.logical_shift_right))
                own.then(nc.vector.tensor_scalar(pij[:, 1, :], pos[:], TOPK - 1, None, ALU.bitwise_and))
                settle()
                cube = [P, 2, TOPK, TOPK]
                own.then(nc.vector.tensor_tensor(eq[:], pij[:].unsqueeze(3).broadcast_to(cube),
                                                 iota.unsqueeze(1).unsqueeze(1).broadcast_to(cube), ALU.is_equal))
                settle()
                own.then(nc.vector.tensor_tensor(eq[:], eq[:], i16[:].unsqueeze(2).broadcast_to(cube), ALU.mult))
                settle()
                own.then(nc.vector.tensor_reduce(eij[:], eq[:], AX.X, ALU.add))
                settle()
                own.then(nc.vector.scalar_tensor_tensor(esum[:], eij[:, 0, :], float(NK), eij[:, 1, :], ALU.mult, ALU.add))
                settle()
                at = turn * PAIR + TOPK * h
                here = bass.ds(at, TOPK)
                nc.vector.tensor_copy(e_all[:, here], esum[:]).then_inc(e_ready, 1)
                dve.wait_ge(bexp_ready, turn * 2 + (h + 1))
                own.then(nc.vector.reciprocal(bsum[:, 1:2], bsum[:, 0:1]))
                settle()
                own.then(nc.vector.tensor_scalar(g_all[:, here], bexp[:], bsum[:, 1:2], None, ALU.mult))
                settle()

            for step in PLAN:
                kind = step[0]
                if kind == "bias":
                    dve.wait_ge(bias_in, 48)
                    src = filled(dve, step)
                    nc.vector.tensor_tensor(biasrow, src[0:NH, 0:ROW], maskrow, ALU.add).then_inc(freed(step), 1)
                    dve.wait_ge(tanh_ready, 1)
                    own.then(nc.vector.tensor_scalar(ctanh[:], ctanh[:], 1.0, 0.5, ALU.add, ALU.mult))
                    own.settle()
                    nc.vector.tensor_tensor(cact[:], ctanh[:], cin[:], ALU.mult).then_inc(cact_ready, 1)
                elif kind == "modc":
                    src = filled(dve, step)
                    nc.vector.tensor_tensor(modc[:], src[:, 0:2 * KC], badac[:], ALU.add).then_inc(freed(step), 1)
                    settle_bank(dve, step)
                    own.then(nc.vector.tensor_scalar(modc[:, KC:], modc[:, KC:], 1.0, None, ALU.add))
                    own.settle()
                    dve.wait_ge(xT_in, 16)
                    for k in range(KC):
                        last = nc.vector.tensor_scalar(hT[:, k, :], xT[:, k, :], modc[:, KC + k:KC + k + 1], modc[:, k:k + 1],
                                                       ALU.mult, ALU.add)
                    last.then_inc(hT_ready, 1)
                elif kind == "wsum":
                    c = step[1]
                    w = chunk(dve, ("ada", c))
                    if c >= 4:
                        filled(dve, ("modc",) if c < 8 else ("modrow", c - 8))
                    dve.wait_ge(cact_ready, 1)
                    part = acc[:, c % 4, :]
                    own.then(nc.vector.tensor_scalar(part, w[:, 0, :], cact[:, 0:1], None, ALU.mult))
                    for k in range(1, KC):
                        own.settle()
                        ins = nc.vector.scalar_tensor_tensor(part, w[:, k, :], cact[:, k:k + 1], part, ALU.mult, ALU.add)
                        if k < KC - 1:
                            own.then(ins)
                    ins.then_inc(acc_ready, 1)
                elif kind == "madd":
                    m = step[1]
                    dve.wait_ge(rows_in, 16)
                    src = filled(dve, ("modrow", m))
                    part = mod[:, m // 2, CH * (m % 2):CH * (m % 2) + CH]
                    one = 0.0 if m // 2 == SH2 else 1.0
                    nc.vector.scalar_tensor_tensor(part, src[:], one, part, ALU.add, ALU.add).then_inc(freed(("modrow", m)), 1)
                elif kind == "S":
                    u = step[1]
                    t, g, par, half = UNITS[u]
                    b0, n, j0 = unit_heads(u)
                    keys = P * (t + 1)
                    settle_bank(dve, ("tflip", j0 // 2))
                    settle_bank(dve, ("tflip", (j0 + n - 1) // 2))
                    src = filled(dve, step)
                    if u == 0:
                        dve.wait_ge(biasrow_out, 16)
                    if u >= 2:
                        b, m = PLACE[("Tr", u - 2)]
                        dve.wait_ge(bank_full[b], m + 1)
                    view = prob[:, u % 2, :].rearrange("p (j k) -> p j k", j=n)
                    nc.vector.scalar_tensor_tensor(view, src[:].rearrange("p (j k) -> p j k", j=n), SCALE,
                                                   toep[:, j0:j0 + n, P * (1 - t):T], ALU.mult, ALU.add).then_inc(freed(step), 1)
                    settle_bank(dve, step)
                    nc.vector.tensor_reduce(negmax[:, u, 0:n], view, AX.X, ALU.max, negate=True).then_inc(negmax_ready, 1)
                elif kind == "PV":
                    u = step[1]
                    t, g, par, half = UNITS[u]
                    b0, n, _ = unit_heads(u)
                    dve.wait_ge(exp_ready, u + 1)
                    own.then(nc.vector.reciprocal(prec[:, u, 0:n], psum_p[:, u, 0:n]))
                    own.settle()
                    src = filled(dve, step)
                    dst = y[:, t, :].rearrange("p (g b z c) -> p g b z c", g=2, z=2, c=HD)[:, g, b0:b0 + n, par, :]
                    nc.vector.tensor_tensor(dst, src[:, 0:HD * n].rearrange("p (j c) -> p j c", j=n),
                                            prec[:, u, 0:n].unsqueeze(2).broadcast_to([P, n, HD]), ALU.mult).then_inc(freed(step), 1)
                elif kind == "ny":
                    t = step[1]
                    dve.wait_ge(sq_ready, t + 1)
                    own.then(nc.vector.reciprocal(ystat[:, t, 2, :], ystat[:, t, 1, :]))
                    own.settle()
                    for g in range(2):
                        half = y[:, t, CH * g:CH * g + CH]
                        nc.vector.tensor_scalar(half, half, ystat[:, t, 2, g:g + 1], None, ALU.mult).then_inc(y_normed, 1)
                elif kind == "yT":
                    t, g = step[1:]
                    dve.wait_ge(gnsk_in, 32)
                    src = filled(dve, step)
                    nc.vector.tensor_tensor(yT[:, t, 4 * g:4 * g + 4, :], src[:].rearrange("p (j c) -> p j c", j=4),
                                            gn[:, 4 * g:4 * g + 4].unsqueeze(2).broadcast_to([P, 4, P]),
                                            ALU.mult).then_inc(freed(step), 1)
                elif kind == "ln1a":
                    t = step[1]
                    dve.wait_ge(x_in, 16)
                    f = [(bank[PLACE[("wo", t, n)][0]][:], (bank_full[PLACE[("wo", t, n)][0]], PLACE[("wo", t, n)][1] + 1),
                          (bank_free[PLACE[("wo", t, n)][0]], PLACE[("wo", t, n)][1] + 1)) for n in range(2)]
                    normalise(t, mod[:, G1, :], f, x[:, t, :], x[:, t, :])
                elif kind == "ln1b":
                    t = step[1]
                    centre(t, x[:, t, :]).then_inc(normed_ready, 1)
                    dve.wait_ge(normed_ready, t + 1)
                    dve.wait_ge(rows2_ready, 1)
                    own.then(nc.vector.tensor_tensor(h2[:, t, :], x[:, t, :], mod[:, SC2, :], ALU.mult))
                    own.settle()
                    nc.vector.tensor_tensor(h2[:, t, :], h2[:, t, :], mod[:, SH2, :], ALU.add).then_inc(h2_ready, 1)
                    dve.wait_ge(h2_ready, t + 1)
                    if t:
                        own.then(nc.vector.tensor_tensor(V_x1[:, t, :], x[:, t, :], lnw[:, 0, :], ALU.mult))
                        own.settle()
                        own.then(nc.vector.tensor_tensor(V_x1[:, t, :], V_x1[:, t, :], lnw[:, 1, :], ALU.add))
                elif kind == "route":
                    head = step[1]
                    dve.wait_ge(consts_in, 16)
                    for z in range(2):
                        settle_bank(dve, ("s", 0, head // 2, z))
                    before = own.n
                    route(head // 2, scores[:, 0, head], head % 2)
                    route_steps = own.n - before
                elif kind == "dots":
                    dots(0, 0, step[1], step[1] + 1)

            for t in range(NT):
                for i in range(4):
                    for z in range(2):
                        settle_bank(dve, ("s", t, i, z))
            base = own.n - 2 * route_steps

            def turn_body(turn, t, routes):
                dots(turn, t, 0, 2)
                if routes:
                    route(turn + 1, scores_of(2 * turn + 2), 0)
                dots(turn, t, 2, 8)
                if routes:
                    route(turn + 1, scores_of(2 * turn + 3), 1)
                dots(turn, t, 8, 16)

            flat = H_s[:].rearrange("p (g z n) -> p g z n", z=2, n=NK)

            def scores_of(head):
                return flat[:, bass.ds(head, 1)].rearrange("p g z n -> p (g z) n")

            def ln2(t):
                f = [(fsum[:, n, :], (f_ready, t + 1), (f_taken, 2 * t + n + 1)) for n in range(2)]
                normalise(NT + t, mod[:, G2, :], f, V_x1[:, t, :], V_x1[:, t, :])
                own.then(centre(NT + t, V_x1[:, t, :]))
                own.settle()
                own.then(nc.vector.tensor_tensor(V_x1[:, t, :], V_x1[:, t, :], lnw[:, 2, :], ALU.mult))
                own.settle()
                nc.vector.tensor_tensor(V_x1[:, t, :], V_x1[:, t, :], lnw[:, 3, :], ALU.add).then_inc(out_ready, 1)

            with dve.Fori(1, TURNS) as turn:
                own.n = turn * (2 * route_steps) + base
                turn_body(turn, 0, True)
            own.n = base + TURNS * 2 * route_steps
            dve.wait_ge(x1_ready, 1)
            ln2(0)
            base = own.n - TURNS * 2 * route_steps
            with dve.Fori(TURNS, NT * TURNS - 1) as turn:
                own.n = turn * (2 * route_steps) + base
                turn_body(turn, 1, True)
            own.n = base + (NT * TURNS - 1) * 2 * route_steps
            turn_body(NT * TURNS - 1, 1, False)
            ln2(1)

        @block.gpsimd
        def _(pool):
            own = Steps(pool, pool_step)
            pool.wait_ge(ln_in, 16)
            for m in range(2, 6):
                settle_bank(pool, ("modrow", m))
            filled(pool, ("tflip", 7))
            own.then(nc.gpsimd.tensor_tensor(H_s[:, 0:D], lnw[:, 1, :], mod[:, SC2, :], ALU.mult))
            own.settle()
            own.then(nc.gpsimd.tensor_tensor(mod[:, SH2, :], mod[:, SH2, :], H_s[:, 0:D], ALU.add))
            own.then(nc.gpsimd.tensor_tensor(mod[:, SC2, :], mod[:, SC2, :], lnw[:, 0, :], ALU.mult))
            own.settle()
            pool.sem_inc(rows2_ready, 1)
            pool.wait_ge(normed_ready, 1)
            filled(pool, ("PV", len(UNITS) - 1))
            own.then(nc.gpsimd.tensor_tensor(V_x1[:, 0, :], x[:, 0, :], lnw[:, 0, :], ALU.mult))
            own.settle()
            nc.gpsimd.tensor_tensor(V_x1[:, 0, :], V_x1[:, 0, :], lnw[:, 1, :], ALU.add).then_inc(x1_ready, 1)

            with pool.Fori(0, NT * TURNS) as turn:
                for h in range(2):
                    pool.wait_ge(e_ready, turn * 2 + (h + 1))
                    pool.sem_inc(pool_gate, 1)
                    nc.gpsimd.tensor_copy(idx[:, h, :], e_all[:, bass.ds(turn * PAIR + TOPK * h, TOPK)]).then_inc(idx_staged, 1)
                    pool.wait_ge(idx_staged, turn * 2 + (h + 1))
                    pool.sem_inc(pool_gate, 1)
                    for k in range(TOPK):
                        s = TOPK * h + k
                        r = s % RING
                        pool.wait_ge(slot_free, turn * PAIR + (s + 1))
                        pool.sem_inc(pool_gate, 1)
                        nc.gpsimd.indirect_dma_start(ring[:, r, :], None, A["experts"],
                                                     bass.IndirectOffsetOnAxis(ap=idx[:, h, k:k + 1], axis=0)).then_inc(slot_in[r], 16)


def shape_constants():
    dist = (T - 1) - np.arange(ROW)
    n = np.maximum(dist, 1).astype(np.float32)
    large = BUCKETS // 2 + (np.log(n / 16) / math.log(2048 / 16) * 16).astype(np.int32)
    bucket = np.where(dist < 16, np.maximum(dist, 0), np.minimum(large, BUCKETS - 1))
    onehot = ((np.arange(BUCKETS)[:, None] == bucket) & (dist >= 0)).astype(np.float32)
    times = sum(((dist % d == 0) & (dist >= 0) & (dist <= w)).astype(np.int32) for w, d in ((128, 1), (512, 4), (2048, 16)))
    moba = np.where(dist >= 0, 0.0, MASKED)
    dil = np.where(times > 0, np.log(np.maximum(times, 1)), MASKED)
    maskrow = np.concatenate([np.tile(moba, (NH // 2, 1)), np.tile(dil, (NH // 2, 1))]).astype(np.float32)
    consts = np.concatenate([np.eye(P), np.eye(P)[::-1], np.tile(np.arange(TOPK), (P, 1))], 1).astype(np.float32)
    return onehot, maskrow, consts


def kernel(**inputs):
    import concourse.bacc as bacc
    from concourse.bass_utils import run_bass_kernel_spmd

    a = {k: np.asarray(v) for k, v in inputs.items()}

    def columns(v):
        return v.reshape(-1, P).T

    def chunks(w):
        return w.reshape(KC, P, -1, CH).transpose(2, 1, 0, 3).reshape(-1, P, KC * CH)

    w = {"ada": chunks(a["w_ada"][0]), "in": chunks(a["w_in"][0]), "out": chunks(a["w_out"][0]), "q": chunks(a["w_q_peer"][0])}
    order = [8 * g + 2 * b + par for g in range(2) for par in range(2) for b in range(4)]
    onehot, maskrow, consts = shape_constants()
    arrays = {
        "c": columns(a["c"][0]),
        "b_ada_c": columns(a["b_ada"][0, :2 * D]),
        "b_ada_r": a["b_ada"][:, 2 * D:],
        "w": np.stack([w[m][c] for m, c in STREAM]),
        "xT": a["x"][0].T.reshape(KC, P, T).transpose(1, 0, 2).reshape(P, KC * T),
        "x": a["x"][0],
        "ln": np.concatenate([a["ln1_g"], a["ln1_b"], a["ln2_g"], a["ln2_b"]], 1),
        "gn": columns(np.concatenate([a["gn_moba"][0], a["gn_dil"][0]])),
        "skT": a["sub_keys"][0].transpose(0, 2, 1).reshape(P, NK),
        "relT": a["rel_bias"][order].T,
        "experts": np.concatenate([a["peer_u"][0], a["peer_v"][0]], 1),
        "onehot": onehot, "maskrow": maskrow, "consts": consts,
    }
    nc = bacc.Bacc("TRN2", target_bir_lowering=False, num_devices=1)
    feeds, A = {}, {}
    for name, v in arrays.items():
        v = np.ascontiguousarray(v)
        feeds[f"in_{name}"] = v
        A[name] = nc.dram_tensor(f"in_{name}", v.shape, mybir.dt.from_np(v.dtype), kind="ExternalInput").ap()
    A["scratch"] = nc.dram_tensor("scratch", (NH, ROW), F32, kind="Internal").ap()
    out = nc.dram_tensor("out_x", (1, T, D), F32, kind="ExternalOutput").ap()
    build(nc, A, out)
    r = run_bass_kernel_spmd(nc, [feeds], core_ids=[0])
    return r.results[0]["out_x"]
```

```python
import math
from contextlib import ExitStack

import numpy as np
import concourse.bass as bass
from concourse import mybir

F32 = mybir.dt.float32
I32 = mybir.dt.int32
U32 = mybir.dt.uint32
ALU = mybir.AluOpType
ACT = mybir.ActivationFunctionType
AX = mybir.AxisListType

P = 128
D = 1024
T = 256
NT = T // P
KC = D // P
HD = 64
NH = 16
CH = 512
BUCKETS = 32
ROW = 384
MASKED = -1e30
ALPHA = 2.0 ** 0.25
EPS = 1e-5
SCALE = HD ** -0.5
PH = 8
NK = 128
TOPK = 16
SLOTS = PH * TOPK
PAIR = 2 * TOPK
TURNS = SLOTS // PAIR
RING = 8
WRING = 4
TAKEN = -3e38
DIAGS = 4
ROUTE_AT = (2, 8)
LN2_AT = (2, 4)
ROUTE_LATE_AT = (6, 10)

STREAM = [("ada", 0), ("ada", 1), ("ada", 2), ("ada", 3), ("in", 0), ("in", 1), ("ada", 4), ("in", 2), ("ada", 5),
          ("ada", 6), ("in", 3), ("ada", 7), ("in", 4), ("ada", 8), ("ada", 9), ("in", 5), ("ada", 10), ("ada", 11),
          ("out", 0), ("q", 0), ("out", 1), ("q", 1)]
LOADED_LAST = ("q", 0)
SLOT_PLACES = [2, 3, 6, 7, 4, 5, 0, 1]
G1, SH2, SC2, G2 = range(4)
UNITS = [(0, 0, 0, 0), (0, 0, 1, 0), (1, 0, 0, 0), (0, 1, 0, 0), (0, 1, 1, 0), (1, 0, 0, 1), (1, 0, 1, 0), (1, 0, 1, 1),
         (1, 1, 0, 0), (1, 1, 0, 1), (1, 1, 1, 0), (1, 1, 1, 1)]
PLAN = (
    [("wsum", 0), ("bias",), ("wsum", 1), ("wsum", 2), ("wsum", 3), ("modc",), ("qk", 0, 0), ("qk", 0, 1), ("qk", 1, 0), ("qk", 1, 1)]
    + [("wsum", 4)] + [("tflip", j) for j in range(4)]
    + [("modrow", 0), ("S", 0), ("S", 1), ("v", 0, 0), ("wsum", 5), ("Tr", 0), ("Tr", 1), ("modrow", 1), ("v", 0, 1),
       ("PV", 0), ("PV", 1), ("S", 2), ("wsum", 6), ("qk", 2, 0), ("Tr", 2), ("modrow", 2), ("qk", 2, 1), ("PV", 2),
       ("wsum", 7), ("qk", 3, 0), ("modrow", 3), ("wsum", 8), ("qk", 3, 1), ("modrow", 4), ("wsum", 9)]
    + [("tflip", j) for j in range(4, 8)]
    + [("modrow", 5), ("S", 3), ("S", 4), ("v", 1, 0), ("wsum", 10), ("Tr", 3), ("Tr", 4), ("S", 5), ("PV", 3), ("PV", 4),
       ("ny", 0), ("modrow", 6), ("Tr", 5), ("S", 6), ("scale_y", 0), ("S", 7), ("PV", 5), ("yT", 0, 0), ("yT", 0, 1),
       ("Tr", 6), ("wsum", 11), ("wo", 0, 0), ("PV", 6), ("Tr", 7), ("S", 8), ("wo", 0, 1), ("modrow", 7), ("PV", 7), ("ln1a", 0),
       ("v", 1, 1), ("Tr", 8), ("S", 9),
       ("PV", 8), ("ln1b", 0), ("Tr", 9), ("S", 10), ("PV", 9), ("hT", 0, 0), ("hT", 0, 1),
       ("Tr", 10), ("S", 11), ("q", 0, 0), ("PV", 10), ("Tr", 11), ("s", 0, 0, 0), ("s", 0, 0, 1), ("PV", 11), ("ny", 1),
       ("route", 0), ("q", 0, 1), ("free", 0), ("scale_y", 1), ("q", 0, 2), ("q", 0, 3), ("yT", 1, 0), ("yT", 1, 1),
       ("s", 0, 1, 0), ("s", 0, 1, 1), ("s", 0, 2, 0), ("s", 0, 2, 1),
       ("wo", 1, 0), ("free", 1), ("dots", 0), ("wo", 1, 1), ("free", 2), ("dots", 1), ("ln1a", 1), ("s", 0, 3, 0), ("s", 0, 3, 1),
       ("slots", 0), ("slots", 1), ("ln1b", 1), ("hT", 1, 0), ("hT", 1, 1), ("dots", 2), ("q", 1, 2), ("slots", 2),
       ("dots", 3), ("slots", 3), ("dots", 4), ("slots", 4), ("q", 1, 3), ("route", 1), ("q", 1, 0), ("dots", 5), ("slots", 5),
       ("dots", 6), ("slots", 6), ("dots", 7), ("q", 1, 1), ("slots", 7), ("dots", 8)]
    + [("s", 1, i, z) for i in range(4) for z in range(2)] + [("slots", 8)]
    + [("route", 2)] + [(kind, p) for p in range(9, 12) for kind in ("dots", "slots")]
    + [("x1", 1)] + [(kind, p) for p in range(12, 14) for kind in ("dots", "slots")]
    + [("route", 3)] + [(kind, p) for p in range(14, 16) for kind in ("dots", "slots")]
)
for _m in range(8):
    PLAN.insert(PLAN.index(("modrow", _m)) + (7 if _m == 0 else 3), ("madd", _m))
CHUNK = {key: n for n, key in enumerate(STREAM)}
STEP_BANKS = 6
NO_FILL = ("ny", "scale_y", "ln1a", "ln1b", "x1", "route", "madd", "wsum", "free", "dots", "slots")
FILLS = [s for s in PLAN if s[0] not in NO_FILL]
LATE = [("wo", t, n) for t in range(NT) for n in range(2)]
PLACE = {s: (n % STEP_BANKS, n // STEP_BANKS) for n, s in enumerate(s for s in FILLS if s not in LATE)}
PLACE |= {s: (STEP_BANKS + n % 2, n // 2) for n, s in enumerate(LATE)}


def unit_heads(u):
    t, g, par, half = UNITS[u]
    b0, n = (0, 4) if t == 0 else (2 * half, 2)
    return b0, n, 8 * g + 4 * par + b0


class Steps:

    def __init__(self, eng, sem):
        self.eng, self.sem, self.n = eng, sem, 0

    def then(self, ins):
        ins.then_inc(self.sem, 1)
        self.n = self.n + 1

    def settle(self):
        self.eng.wait_ge(self.sem, self.n)

    def settle_here(self, gate):
        self.settle()
        self.eng.sem_inc(gate, 1)


def build(nc, A, out):
    ctx = ExitStack()
    with ctx:
        def sb(name, shape, dt=F32):
            return ctx.enter_context(nc.sbuf_tensor(name, shape, dt))

        def sem(name):
            return ctx.enter_context(nc.semaphore(name))

        ring = sb("ring", [P, RING, 2 * D])
        wring = ring[:].rearrange("p r c -> p (r c)").rearrange("p (w k n) -> p w k n", w=WRING, k=KC)
        xT_y = sb("xT_y", [P, KC * T])
        xT = xT_y[:].rearrange("p (k t) -> p k t", k=KC)
        y = xT_y[:].rearrange("p (t c) -> p t c", t=NT)
        hT_yT = sb("hT_yT", [P, KC * T])
        hT = hT_yT[:].rearrange("p (k t) -> p k t", k=KC)
        x = sb("x", [P, NT, D])
        QT_h2T = sb("QT_h2T", [P, KC * T])
        QT = QT_h2T[:].rearrange("p (b t) -> p b t", b=KC)
        h2T = QT_h2T[:].rearrange("p (t k c) -> p t k c", t=NT, k=KC)
        KT_qT = sb("KT_qT", [P, KC * T])
        KT = KT_qT[:].rearrange("p (b t) -> p b t", b=KC)
        qT = KT_qT[:].rearrange("p (t h c) -> p t h c", t=NT, h=PH)
        V_x1 = sb("V_x1", [P, NT, D])
        H_s = sb("H_s", [P, NH * T])
        hankel = H_s[:].rearrange("p (h k) -> p h k", h=NH)
        yT = [part.rearrange("p (k c) -> p k c", k=KC) for part in (H_s[:, D:2 * D], hT_yT[:, 0:D])]
        scores = H_s[:].rearrange("p (t h z n) -> p t h z n", t=NT, h=PH, z=2)
        T_h2 = sb("T_h2", [P, NH * T])
        toep = T_h2[:].rearrange("p (h k) -> p h k", h=NH)
        h2 = T_h2[:, 0:NT * D].rearrange("p (t c) -> p t c", t=NT)
        mod = sb("mod", [P, 4, D])
        lnw = sb("lnw", [P, 4, D])
        halves = {"high": (T_h2[:, NT * D:], H_s[:, NT * D:])}
        acc = sb("acc", [P, 4, CH])
        probs = sb("probs", [P, 4 * CH])
        prob = probs[:, 0:2 * CH].rearrange("p (u k) -> p u k", u=2)
        probT = probs[:, 2 * CH:].rearrange("p (u k) -> p u k", u=2)
        halves["low"] = (probs[:], xT_y[:])
        onehot = probT[0:BUCKETS, 0, 0:ROW]
        maskrow = probT[0:NH, 1, 0:ROW]
        biasrow = prob[0:NH, 0, 0:ROW]
        relT = sb("relT", [BUCKETS, NH])
        consts = sb("consts", [P, 2 * P + TOPK])
        ident, flip, iota = consts[:, 0:P], consts[:, P:2 * P], consts[:, 2 * P:2 * P + TOPK]
        ones = sb("ones", [P, P])
        zeros = sb("zeros", [P, P])
        cin = sb("cin", [P, KC])
        ctanh = sb("ctanh", [P, KC])
        cact = sb("cact", [P, KC])
        badac = sb("badac", [P, 2 * KC])
        modc = sb("modc", [P, 2 * KC])
        gn = sb("gn", [P, KC])
        skT = sb("skT", [P, NK])
        epsc = sb("epsc", [P, 1])
        spare = sb("spare", [P, 1])
        negmax = sb("negmax", [P, len(UNITS), 4])
        psum_p = sb("psum_p", [P, len(UNITS), 4])
        prec = sb("prec", [P, len(UNITS), 4])
        ystat = sb("ystat", [P, NT, 3, 2])
        lnst = sb("lnst", [P, 2 * NT, 6])
        junk = sb("junk", [P, D], mybir.dt.bfloat16)
        diag = sb("diag", [P, DIAGS, P])
        swork = sb("swork", [P, 2, 2, NK])
        v16 = sb("v16", [P, 2, TOPK])
        i16 = sb("i16", [P, 2, TOPK], U32)
        cand = acc[:, 2, :].rearrange("p (i n) -> p i n", i=2)
        best = sb("best", [P, TOPK])
        pos = sb("pos", [P, TOPK], U32)
        pij = sb("pij", [P, 2, TOPK], U32)
        eq = acc[:, 3, :].rearrange("p (z k n) -> p z k n", z=2, k=TOPK)
        eij = sb("eij", [P, 2, TOPK])
        esum = sb("esum", [P, TOPK])
        bdiff = sb("bdiff", [P, TOPK])
        bexp = sb("bexp", [P, TOPK])
        bsum = sb("bsum", [P, 2])
        e_all = sb("e_all", [P, NT * SLOTS], I32)
        g_all = sb("g_all", [P, NT * SLOTS])
        pre = sb("pre", [P, PAIR])
        gel = sb("gel", [P, PAIR])
        idx = sb("idx", [P, 2, TOPK], I32)
        bank = [ctx.enter_context(nc.psum_tensor(f"bank{i}", [P, CH], F32))[:] for i in range(8)]

        bank_full = [sem(f"bank_full{i}") for i in range(len(bank))]
        bank_free = [sem(f"bank_free{i}") for i in range(len(bank))]
        w_in = [[sem(f"w_in{i}_{z}") for z in range(2)] for i in range(WRING)]
        c_in, badac_in, bias_in, xT_in, consts_in, x_in, rows_in, ln_in, gnsk_in = (sem(n) for n in (
            "c_in", "badac_in", "bias_in", "xT_in", "consts_in", "x_in", "rows_in", "ln_in", "gnsk_in"))
        wq_in = {"high": sem("wq_high_in"), "low": sem("wq_low_in")}
        biasrow_out, hankel_in = sem("biasrow_out"), sem("hankel_in")
        tanh_ready, cact_ready, hT_ready = sem("tanh_ready"), sem("cact_ready"), sem("hT_ready")
        acc_ready = sem("acc_ready")
        negmax_ready, exp_ready = sem("negmax_ready"), sem("exp_ready")
        sq_ready, y_normed = sem("sq_ready"), sem("y_normed")
        mean_ready, std_ready = sem("mean_ready"), sem("std_ready")
        inverse_ready, x1_ready, h2_ready, rows2_ready = sem("inverse_ready"), sem("x1_ready"), sem("h2_ready"), sem("rows2_ready")
        set_ready = sem("set_ready")
        dve_step, act_step, pool_step = sem("dve_step"), sem("act_step"), sem("pool_step")
        dve_gate, pool_gate = sem("dve_gate"), sem("pool_gate")
        best_ready, bexp_ready, e_ready = sem("best_ready"), sem("bexp_ready"), sem("e_ready")
        idx_staged = sem("idx_staged")
        slot_in = [sem(f"slot_in{i}") for i in range(RING)]
        slot_free = sem("slot_free")
        dots_ready, gelu_ready, diag_ready = sem("dots_ready"), sem("gelu_ready"), sem("diag_ready")
        f_ready, f_taken, out_ready, out_done = sem("f_ready"), sem("f_taken"), sem("out_ready"), sem("out_done")

        def tile_sum(t):
            return (bank[STEP_BANKS:], bank[:2])[t]

        def filled(eng, step):
            b, n = PLACE[step]
            eng.wait_ge(bank_full[b], n + 1)
            return bank[b]

        def freed(step):
            return bank_free[PLACE[step][0]]

        def settle_bank(eng, step):
            b, n = PLACE[step]
            eng.wait_ge(bank_free[b], n + 1)

        def arrived(eng, n, z):
            eng.wait_ge(w_in[n % WRING][z], 16 * (n // WRING + 1))

        def chunk(eng, key):
            n = CHUNK[key]
            arrived(eng, n, 0)
            arrived(eng, n, 1)
            return wring[:, n % WRING]

        def query_weights(eng, t, i):
            if t == 0 and i < 2:
                return lambda k, w=chunk(eng, ("q", 0)): w[:, k, :]
            part = "low" if i < 2 else "high"
            eng.wait_ge(wq_in[part], 32)
            w = [half.rearrange("p (k n) -> p k n", n=CH) for half in halves[part]]
            return lambda k: w[k // (KC // 2)][:, k % (KC // 2), :]

        def chunk_used(eng, key):
            m, c = key
            if m == "ada":
                eng.wait_ge(acc_ready, c + 1)
            elif m == "in":
                filled(eng, (("qk", 0, 1), ("qk", 1, 1), ("v", 0, 1), ("qk", 2, 1), ("qk", 3, 1), ("v", 1, 1))[c])
            else:
                raise ValueError("nothing follows this chunk")

        def parts(turn, p):
            if isinstance(turn, int) and turn == NT * TURNS - 1 and p == PAIR // 2 - 1:
                return slice(2 * p, 2 * p + 1), slice(2 * p + 1, 2 * p + 2)
            return (slice(2 * p, 2 * p + 2),)

        block = ctx.enter_context(nc.Block())

        @block.sync
        def _(sp):
            sp.dma_start(cin[:], A["c"]).then_inc(c_in, 16)

            def load(n):
                if n >= WRING:
                    chunk_used(sp, STREAM[n - WRING])
                src = A["w"][n].rearrange("p (k n) -> p k n", k=KC)
                for z in range(2):
                    half = slice(KC // 2 * z, KC // 2 * (z + 1))
                    sp.dma_start(wring[:, n % WRING, half], src[:, half]).then_inc(w_in[n % WRING][z], 16)

            load(0)
            sp.dma_start(badac[:], A["b_ada_c"]).then_inc(badac_in, 16)
            for name, dst in (("relT", relT[:]), ("onehot", onehot), ("maskrow", maskrow)):
                sp.dma_start(dst, A[name]).then_inc(bias_in, 16)
            load(1)
            sp.dma_start(consts[:], A["consts"]).then_inc(consts_in, 16)
            load(2)
            load(3)
            sp.dma_start(xT, A["xT"].rearrange("p (k t) -> p k t", k=KC)).then_inc(xT_in, 16)
            load(4)
            load(5)
            settle_bank(sp, ("bias",))
            sp.dma_start(A["scratch"], biasrow).then_inc(biasrow_out, 16)
            sp.wait_ge(biasrow_out, 16)
            shifts = bass.AP(A["scratch"].tensor, 0, [[1, P], [ROW, NH], [1, T]])
            sp.dma_start(hankel, shifts).then_inc(hankel_in, 16)
            for n in range(WRING + 2, len(STREAM) - 1):
                if STREAM[n] != LOADED_LAST:
                    load(n)
                if n == 9:
                    sp.dma_start(mod[:].rearrange("p r c -> p (r c)"), A["b_ada_r"].broadcast_to([P, 4 * D])).then_inc(rows_in, 16)
                if n == 11:
                    sp.dma_start(x[:], A["x"].rearrange("(t p) c -> p t c", p=P)).then_inc(x_in, 16)
                    sp.dma_start(gn[:], A["gn"]).then_inc(gnsk_in, 16)
                    sp.dma_start(skT[:], A["skT"]).then_inc(gnsk_in, 16)
                if n == 13:
                    sp.dma_start(lnw[:].rearrange("p r c -> p (r c)"), A["ln"].broadcast_to([P, 4 * D])).then_inc(ln_in, 16)
            load(CHUNK[LOADED_LAST])

            def load_half(part, z):
                n = CHUNK[("q", 1 if part == "high" else 0)]
                sp.dma_start(halves[part][z], A["w"][n, :, 2 * D * z:2 * D * z + 2 * D]).then_inc(wq_in[part], 16)

            filled(sp, ("tflip", 7))
            load_half("high", 1)
            settle_bank(sp, ("S", len(UNITS) - 1))
            load_half("high", 0)
            filled(sp, ("PV", len(UNITS) - 1))
            load_half("low", 0)
            filled(sp, ("yT", 1, 0))
            filled(sp, ("yT", 1, 1))
            load_half("low", 1)
            for t in range(NT):
                for n in range(2):
                    half = slice(CH * n, CH * n + CH)
                    sp.wait_ge(out_ready, 2 * t + n + 1)
                    sp.dma_start(out[0, P * t:P * t + P, half], V_x1[:, t, half]).then_inc(out_done, 16)
            sp.wait_ge(out_done, 16 * 2 * NT)

        @block.tensor
        def _(pe):
            def open_bank(step):
                b, n = PLACE[step]
                if n:
                    pe.wait_ge(bank_free[b], n)
                return bank[b], bank_full[b]

            def product(dst, lhs, rhs, n=KC):
                for k in range(n):
                    last = nc.tensor.matmul(dst, lhs(k), rhs(k), start=(k == 0), stop=(k == n - 1))
                return last

            def slot(turn, t, s, opens=False):
                pe.wait_ge(diag_ready, turn * PAIR + (s + 1))
                for n in range(2):
                    last = nc.tensor.matmul(tile_sum(t)[n], diag[:, s % DIAGS, :],
                                            ring[:, SLOT_PLACES[s % RING], D + CH * n:D + CH * n + CH], start=opens, stop=False)
                last.then_inc(slot_free, 1)

            for step in PLAN:
                kind = step[0]
                if kind == "slots":
                    for s in (2 * step[1], 2 * step[1] + 1):
                        if s == 0:
                            for late in LATE[-2:]:
                                settle_bank(pe, late)
                        slot(0, 0, s, opens=(s == 0))
                if kind in NO_FILL:
                    continue
                dst, full = open_bank(step)
                if kind == "bias":
                    pe.wait_ge(bias_in, 48)
                    nc.tensor.matmul(dst[0:NH, 0:ROW], relT[:], onehot, start=True, stop=True).then_inc(full, 1)
                elif kind == "modc":
                    pe.wait_ge(set_ready, 1)
                    for c in range(4):
                        pe.wait_ge(acc_ready, c + 1)
                        for j in range(4):
                            last = nc.tensor.matmul(dst[:, 4 * c + j:4 * c + j + 1], acc[:, c, P * j:P * j + P],
                                                    ones[:, 0:1], start=True, stop=True)
                    last.then_inc(full, 1)
                elif kind == "qk":
                    c, i = step[1:]
                    key = ("in", (0, 1, 3, 4)[c])
                    n = CHUNK[key]
                    w = wring[:, n % WRING]
                    for j in range(2):
                        for k in range(KC):
                            if c == 0 and i == 0 and j == 0:
                                pe.wait_ge(hT_ready, k + 1)
                            if j == 0 and k % (KC // 2) == 0:
                                arrived(pe, n, 2 * k // KC)
                            last = nc.tensor.matmul(dst[:, T * j:T * j + T], w[:, k, P * (2 * i + j):P * (2 * i + j) + P],
                                                    hT[:, k, :], start=(k == 0), stop=(k == KC - 1))
                    last.then_inc(full, 1)
                elif kind == "v":
                    g, t = step[1:]
                    w = chunk(pe, ("in", 2 + 3 * g))
                    product(dst[:], lambda k: hT[:, k, P * t:P * t + P], lambda k: w[:, k, :]).then_inc(full, 1)
                elif kind == "tflip":
                    pe.wait_ge(consts_in, 16)
                    pe.wait_ge(hankel_in, 16)
                    nc.tensor.matmul(dst[:], flip, H_s[:, CH * step[1]:CH * step[1] + CH], start=True, stop=True).then_inc(full, 1)
                elif kind == "modrow":
                    pe.wait_ge(set_ready, 1)
                    pe.wait_ge(acc_ready, step[1] + 5)
                    nc.tensor.matmul(dst[:], ones[:], acc[:, step[1] % 4, :], start=True, stop=True).then_inc(full, 1)
                elif kind == "S":
                    t, g, par, half = UNITS[step[1]]
                    b0, n, _ = unit_heads(step[1])
                    for i in range(2):
                        settle_bank(pe, ("qk", 2 * g, i))
                        settle_bank(pe, ("qk", 2 * g + 1, i))
                    r = slice(HD * par, HD * par + HD)
                    keys = P * (t + 1)
                    for j in range(n):
                        last = nc.tensor.matmul(dst[:, keys * j:keys * j + keys], QT[r, 4 * g + b0 + j, P * t:P * t + P],
                                                KT[r, 4 * g + b0 + j, 0:keys], start=True, stop=True)
                    last.then_inc(full, 1)
                elif kind == "Tr":
                    pe.wait_ge(exp_ready, step[1] + 1)
                    pe.wait_ge(consts_in, 16)
                    for j in range(4):
                        last = nc.tensor.transpose(dst[:, P * j:P * j + P], prob[:, step[1] % 2, P * j:P * j + P], ident)
                    last.then_inc(full, 1)
                elif kind == "PV":
                    t, g, par, half = UNITS[step[1]]
                    b0, n, _ = unit_heads(step[1])
                    settle_bank(pe, ("Tr", step[1]))
                    for tt in range(t + 1):
                        settle_bank(pe, ("v", g, tt))
                    for j in range(n):
                        c = D // 2 * g + P * (b0 + j) + HD * par
                        for kt in range(t + 1):
                            at = P * ((t + 1) * j + kt)
                            last = nc.tensor.matmul(dst[:, HD * j:HD * j + HD], probT[:, step[1] % 2, at:at + P],
                                                    V_x1[:, kt, c:c + HD], start=(kt == 0), stop=(kt == t))
                    last.then_inc(full, 1)
                elif kind == "yT":
                    t, g = step[1:]
                    pe.wait_ge(y_normed, 2 * t + 2)
                    for j in range(4):
                        last = nc.tensor.transpose(dst[:, P * j:P * j + P], y[:, t, P * (4 * g + j):P * (4 * g + j) + P], ident)
                    last.then_inc(full, 1)
                elif kind == "wo":
                    t, n = step[1:]
                    w = chunk(pe, ("out", n))
                    settle_bank(pe, ("yT", t, 0))
                    settle_bank(pe, ("yT", t, 1))
                    product(dst[:], lambda k: yT[t][:, k, :], lambda k: w[:, k, :]).then_inc(full, 1)
                elif kind == "hT":
                    t, i = step[1:]
                    pe.wait_ge(h2_ready, t + 1)
                    for j in range(4):
                        last = nc.tensor.transpose(dst[:, P * j:P * j + P], h2[:, t, P * (4 * i + j):P * (4 * i + j) + P], ident)
                    last.then_inc(full, 1)
                elif kind == "q":
                    t, i = step[1:]
                    w = query_weights(pe, t, i)
                    settle_bank(pe, ("hT", t, 0))
                    settle_bank(pe, ("hT", t, 1))
                    for j in range(2):
                        c = P * (2 * (i % 2) + j)
                        last = product(dst[:, P * j:P * j + P], lambda k: w(k)[:, c:c + P], lambda k: h2T[:, t, k, :])
                    last.then_inc(full, 1)
                elif kind == "s":
                    t, i, z = step[1:]
                    pe.wait_ge(gnsk_in, 32)
                    settle_bank(pe, ("q", t, i))
                    r = slice(HD * z, HD * z + HD)
                    for j in range(2):
                        last = nc.tensor.matmul(dst[:, P * j:P * j + P], qT[r, t, 2 * i + j, :], skT[r, :], start=True, stop=True)
                    last.then_inc(full, 1)

            def close(t):
                for n in range(2):
                    last = nc.tensor.matmul(tile_sum(t)[n][:, 0:1], zeros[:], zeros[:, 0:1], start=False, stop=True)
                last.then_inc(f_ready, 1)

            with pe.Fori(1, TURNS) as turn:
                for s in range(PAIR):
                    slot(turn, 0, s)
            close(0)
            for s in range(PAIR):
                if s == 0:
                    for b in range(2):
                        pe.wait_ge(bank_free[b], sum(1 for place in PLACE.values() if place[0] == b))
                slot(TURNS, 1, s, opens=(s == 0))
            with pe.Fori(TURNS + 1, NT * TURNS) as turn:
                for s in range(PAIR):
                    slot(turn, 1, s)
            close(1)

        @block.scalar
        def _(act):
            own = Steps(act, act_step)
            act.wait_ge(set_ready, 1)
            act.wait_ge(c_in, 16)
            nc.scalar.activation(ctanh[:], cin[:], ACT.Tanh, scale=0.5).then_inc(tanh_ready, 1)

            def route_exp(head):
                act.wait_ge(best_ready, head + 1)
                nc.scalar.activation(bexp[:], bdiff[:], ACT.Exp, accum_out=bsum[:, 0:1]).then_inc(bexp_ready, 1)

            def gelus(turn, p0, p1):
                for p in range(p0, p1):
                    for n, part in enumerate(parts(turn, p)):
                        act.wait_ge(dots_ready, turn * (PAIR // 2) + (p + n + 1))
                        nc.scalar.activation(gel[:, part], pre[:, part], ACT.Gelu).then_inc(gelu_ready, 1)

            def load_sqrt():
                own.settle()
                own.then(nc.scalar.activation(spare[:], epsc[:], ACT.Sqrt))

            def evacuate(step, dst, src):
                nc.scalar.copy(dst, src).then_inc(freed(step), 1)

            def deviation(i, z):
                load_sqrt()
                act.wait_ge(mean_ready, i + 1)
                own.settle()
                own.then(nc.scalar.activation(junk[:], z, ACT.Square, bias=lnst[:, i, 2:3], accum_out=lnst[:, i, 3:4]))
                own.settle()
                nc.scalar.activation(lnst[:, i, 4:5], lnst[:, i, 3:4], ACT.Sqrt, bias=epsc[:], scale=1.0 / D).then_inc(std_ready, 1)

            for step in PLAN:
                kind = step[0]
                if kind == "tflip":
                    src = filled(act, step)
                    evacuate(step, T_h2[:, CH * step[1]:CH * step[1] + CH], src[:])
                elif kind == "qk":
                    c, i = step[1:]
                    dst = (QT, KT)[c % 2][:, 4 * (c // 2) + 2 * i:4 * (c // 2) + 2 * i + 2, :]
                    evacuate(step, dst, filled(act, step)[:].rearrange("p (j t) -> p j t", j=2))
                elif kind == "v":
                    g, t = step[1:]
                    evacuate(step, V_x1[:, t, CH * g:CH * g + CH], filled(act, step)[:])
                elif kind == "S":
                    t = UNITS[step[1]][0]
                    _, n, _ = unit_heads(step[1])
                    keys = P * (t + 1)
                    act.wait_ge(negmax_ready, step[1] + 1)
                    for j in range(n):
                        part = prob[:, step[1] % 2, keys * j:keys * j + keys]
                        last = nc.scalar.activation(part, part, ACT.Exp, bias=negmax[:, step[1], j:j + 1],
                                                    accum_out=psum_p[:, step[1], j:j + 1])
                    last.then_inc(exp_ready, 1)
                elif kind == "Tr":
                    if step[1] >= 2:
                        b, n = PLACE[("PV", step[1] - 2)]
                        act.wait_ge(bank_full[b], n + 1)
                    evacuate(step, probT[:, step[1] % 2, :], filled(act, step)[:])
                elif kind == "ny":
                    t = step[1]
                    load_sqrt()
                    for u, unit in enumerate(UNITS):
                        if unit[0] == t:
                            settle_bank(act, ("PV", u))
                    for g in range(2):
                        own.then(nc.scalar.activation(junk[:, 0:CH], y[:, t, CH * g:CH * g + CH], ACT.Square,
                                                      accum_out=ystat[:, t, 0, g:g + 1]))
                        own.settle()
                    nc.scalar.activation(ystat[:, t, 1, :], ystat[:, t, 0, :], ACT.Sqrt, bias=epsc[:],
                                         scale=1.0 / CH).then_inc(sq_ready, 1)
                elif kind == "ln1a":
                    t = step[1]
                    deviation(t, x[:, t, :])
                elif kind == "hT":
                    t, i = step[1:]
                    evacuate(step, h2T[:, t, 4 * i:4 * i + 4, :], filled(act, step)[:].rearrange("p (j c) -> p j c", j=4))
                elif kind == "q":
                    t, i = step[1:]
                    evacuate(step, qT[:, t, 2 * i:2 * i + 2, :], filled(act, step)[:, 0:2 * P].rearrange("p (j c) -> p j c", j=2))
                elif kind == "s":
                    t, i, z = step[1:]
                    evacuate(step, scores[:, t, 2 * i:2 * i + 2, z, :], filled(act, step)[:, 0:2 * P].rearrange("p (j n) -> p j n", j=2))
                elif kind == "route":
                    route_exp(step[1])
                elif kind == "free":
                    if step[1] == 0:
                        act.wait_ge(acc_ready, 12)
                        filled(act, ("q", 0, 1))
                        act.sem_inc(slot_free, RING // 2)
                    else:
                        filled(act, ("wo", 1, step[1] - 1))
                        act.sem_inc(slot_free, RING // 4)
                elif kind == "dots":
                    gelus(0, step[1], step[1] + 1)

            def turn_body(turn, between):
                for p in range(PAIR // 2):
                    if p in between:
                        between[p]()
                    gelus(turn, p, p + 1)

            def routes(turn, p0, p1):
                return {p0: lambda: route_exp(2 * turn + 2), p1: lambda: route_exp(2 * turn + 3)}

            with act.Fori(1, TURNS) as turn:
                turn_body(turn, routes(turn, *ROUTE_AT))
            turn_body(TURNS, {LN2_AT[0]: lambda: deviation(NT, V_x1[:, 0, :])} | routes(TURNS, *ROUTE_LATE_AT))
            with act.Fori(TURNS + 1, NT * TURNS - 1) as turn:
                turn_body(turn, routes(turn, *ROUTE_AT))
            turn_body(NT * TURNS - 1, {})
            deviation(NT + 1, V_x1[:, 1, :])

        @block.vector
        def _(dve):
            own = Steps(dve, dve_step)
            nc.vector.memset(ones[:], 1.0)
            nc.vector.memset(zeros[:], 0.0)
            nc.vector.memset(epsc[:], EPS).then_inc(set_ready, 1)
            dve.wait_ge(tanh_ready, 1)
            own.then(nc.vector.tensor_scalar(ctanh[:], ctanh[:], 1.0, 0.5, ALU.add, ALU.mult))
            own.settle()
            nc.vector.tensor_tensor(cact[:], ctanh[:], cin[:], ALU.mult).then_inc(cact_ready, 1)

            def add_residual(i, gate, f, res, z):
                halves = [slice(CH * n, CH * n + CH) for n in range(2)]
                own.settle()
                for n in range(2):
                    src, ready, taken = f[n]
                    dve.wait_ge(*ready)
                    nc.vector.tensor_tensor(acc[:, n, :], src, gate[:, halves[n]], ALU.mult).then_inc(taken[0], 1)
                for n in range(2):
                    dve.wait_ge(*f[n][2])
                    own.then(nc.vector.scalar_tensor_tensor(z[:, halves[n]], res[:, halves[n]], ALPHA,
                                                            acc[:, n, :], ALU.mult, ALU.add, accum_out=lnst[:, i, n:n + 1]))
                own.settle()
                nc.vector.tensor_scalar(lnst[:, i, 2:3], lnst[:, i, 0:1], lnst[:, i, 1:2], -1.0 / D,
                                        ALU.add, ALU.mult).then_inc(mean_ready, 1)

            def centre(i, z, gain, dst):
                dve.wait_ge(mean_ready, i + 1)
                own.then(nc.vector.scalar_tensor_tensor(dst, z, lnst[:, i, 2:3], gain, ALU.add, ALU.mult))

            def inverse(i):
                dve.wait_ge(std_ready, i + 1)
                nc.vector.reciprocal(lnst[:, i, 5:6], lnst[:, i, 4:5]).then_inc(inverse_ready, 1)

            def scale(i, centred, offset, dst):
                own.settle()
                dve.wait_ge(inverse_ready, i + 1)
                return nc.vector.scalar_tensor_tensor(dst, centred, lnst[:, i, 5:6], offset, ALU.mult, ALU.add)

            def dots(turn, t, p0, p1):
                for p, (n, part) in ((p, at) for p in range(p0, p1) for at in enumerate(parts(turn, p))):
                    for s in range(part.start, part.stop):
                        r = SLOT_PLACES[s % RING]
                        dve.wait_ge(slot_in[r], turn * (16 * PAIR // RING) + 16 * (s // RING + 1))
                        last = nc.vector.tensor_tensor_reduce(ring[:, r, 0:D], ring[:, r, 0:D], h2[:, t, :], 1.0, 0.0,
                                                              ALU.mult, ALU.add, pre[:, s:s + 1])
                    last.then_inc(dots_ready, 1)
                    dve.wait_ge(gelu_ready, turn * (PAIR // 2) + (p + n + 1))
                    for s in range(part.start, part.stop):
                        dve.wait_ge(slot_free, turn * PAIR + (RING + s - DIAGS + 1))
                        nc.vector.tensor_scalar(diag[:, s % DIAGS, :], ident, gel[:, s:s + 1],
                                                g_all[:, bass.ds(turn * PAIR + s, 1)], ALU.mult, ALU.mult).then_inc(diag_ready, 1)

            def route(turn, both, h):
                def settle():
                    own.settle_here(dve_gate)

                settle()
                own.then(nc.vector.tensor_copy(swork[:, 0], both))
                settle()
                for z in range(2):
                    own.then(nc.vector.max(v16[:, z, 0:8], swork[:, 0, z, :]))
                settle()
                for z in range(2):
                    own.then(nc.vector.max_index(i16[:, z, 0:8], v16[:, z, 0:8], swork[:, 0, z, :]))
                    own.then(nc.vector.match_replace(swork[:, 1, z, :], v16[:, z, 0:8], swork[:, 0, z, :], TAKEN))
                settle()
                for z in range(2):
                    own.then(nc.vector.max(v16[:, z, 8:16], swork[:, 1, z, :]))
                settle()
                for z in range(2):
                    own.then(nc.vector.max_index(i16[:, z, 8:16], v16[:, z, 8:16], swork[:, 1, z, :]))
                square = [P, TOPK, TOPK]
                own.then(nc.vector.tensor_tensor(cand[:, 0, :].rearrange("p (i j) -> p i j", i=TOPK),
                                                 v16[:, 0, :].unsqueeze(2).broadcast_to(square),
                                                 v16[:, 1, :].unsqueeze(1).broadcast_to(square), ALU.add))
                settle()
                own.then(nc.vector.max(best[:, 0:8], cand[:, 0, :]))
                settle()
                own.then(nc.vector.max_index(pos[:, 0:8], best[:, 0:8], cand[:, 0, :]))
                own.then(nc.vector.match_replace(cand[:, 1, :], best[:, 0:8], cand[:, 0, :], TAKEN))
                settle()
                own.then(nc.vector.max(best[:, 8:16], cand[:, 1, :]))
                settle()
                nc.vector.tensor_scalar(bdiff[:], best[:], best[:, 0:1], None, ALU.subtract).then_inc(best_ready, 1)
                own.then(nc.vector.max_index(pos[:, 8:16], best[:, 8:16], cand[:, 1, :]))
                settle()
                own.then(nc.vector.tensor_scalar(pij[:, 0, :], pos[:], 4, None, ALU.logical_shift_right))
                own.then(nc.vector.tensor_scalar(pij[:, 1, :], pos[:], TOPK - 1, None, ALU.bitwise_and))
                settle()
                cube = [P, 2, TOPK, TOPK]
                own.then(nc.vector.tensor_tensor(eq[:], pij[:].unsqueeze(3).broadcast_to(cube),
                                                 iota.unsqueeze(1).unsqueeze(1).broadcast_to(cube), ALU.is_equal))
                settle()
                own.then(nc.vector.tensor_tensor(eq[:], eq[:], i16[:].unsqueeze(2).broadcast_to(cube), ALU.mult))
                settle()
                own.then(nc.vector.tensor_reduce(eij[:], eq[:], AX.X, ALU.add))
                settle()
                own.then(nc.vector.scalar_tensor_tensor(esum[:], eij[:, 0, :], float(NK), eij[:, 1, :], ALU.mult, ALU.add))
                settle()
                at = turn * PAIR + TOPK * h
                here = bass.ds(at, TOPK)
                nc.vector.tensor_copy(e_all[:, here], esum[:]).then_inc(e_ready, 1)
                dve.wait_ge(bexp_ready, turn * 2 + (h + 1))
                own.then(nc.vector.reciprocal(bsum[:, 1:2], bsum[:, 0:1]))
                settle()
                own.then(nc.vector.tensor_scalar(g_all[:, here], bexp[:], bsum[:, 1:2], None, ALU.mult))
                settle()

            for step in PLAN:
                kind = step[0]
                if kind == "bias":
                    dve.wait_ge(bias_in, 48)
                    src = filled(dve, step)
                    nc.vector.tensor_tensor(biasrow, src[0:NH, 0:ROW], maskrow, ALU.add).then_inc(freed(step), 1)
                elif kind == "modc":
                    dve.wait_ge(badac_in, 16)
                    src = filled(dve, step)
                    nc.vector.tensor_tensor(modc[:], src[:, 0:2 * KC], badac[:], ALU.add).then_inc(freed(step), 1)
                    settle_bank(dve, step)
                    own.then(nc.vector.tensor_scalar(modc[:, KC:], modc[:, KC:], 1.0, None, ALU.add))
                    own.settle()
                    dve.wait_ge(xT_in, 16)
                    for k in range(KC):
                        nc.vector.tensor_scalar(hT[:, k, :], xT[:, k, :], modc[:, KC + k:KC + k + 1], modc[:, k:k + 1],
                                                ALU.mult, ALU.add).then_inc(hT_ready, 1)
                elif kind == "wsum":
                    c = step[1]
                    n = CHUNK[("ada", c)]
                    w = wring[:, n % WRING]
                    arrived(dve, n, 0)
                    if c >= 4:
                        filled(dve, ("modc",) if c < 8 else ("modrow", c - 8))
                    dve.wait_ge(cact_ready, 1)
                    part = acc[:, c % 4, :]
                    own.then(nc.vector.tensor_scalar(part, w[:, 0, :], cact[:, 0:1], None, ALU.mult))
                    for k in range(1, KC):
                        if k == KC // 2:
                            arrived(dve, n, 1)
                        own.settle()
                        ins = nc.vector.scalar_tensor_tensor(part, w[:, k, :], cact[:, k:k + 1], part, ALU.mult, ALU.add)
                        if k < KC - 1:
                            own.then(ins)
                    ins.then_inc(acc_ready, 1)
                elif kind == "madd":
                    m = step[1]
                    dve.wait_ge(rows_in, 16)
                    src = filled(dve, ("modrow", m))
                    part = mod[:, m // 2, CH * (m % 2):CH * (m % 2) + CH]
                    one = 0.0 if m // 2 == SH2 else 1.0
                    nc.vector.scalar_tensor_tensor(part, src[:], one, part, ALU.add, ALU.add).then_inc(freed(("modrow", m)), 1)
                elif kind == "S":
                    u = step[1]
                    t, g, par, half = UNITS[u]
                    b0, n, j0 = unit_heads(u)
                    keys = P * (t + 1)
                    settle_bank(dve, ("tflip", j0 // 2))
                    settle_bank(dve, ("tflip", (j0 + n - 1) // 2))
                    src = filled(dve, step)
                    if u == 0:
                        dve.wait_ge(biasrow_out, 16)
                    if u >= 2:
                        b, m = PLACE[("Tr", u - 2)]
                        dve.wait_ge(bank_full[b], m + 1)
                    view = prob[:, u % 2, :].rearrange("p (j k) -> p j k", j=n)
                    nc.vector.scalar_tensor_tensor(view, src[:].rearrange("p (j k) -> p j k", j=n), SCALE,
                                                   toep[:, j0:j0 + n, P * (1 - t):T], ALU.mult, ALU.add).then_inc(freed(step), 1)
                    settle_bank(dve, step)
                    nc.vector.tensor_reduce(negmax[:, u, 0:n], view, AX.X, ALU.max, negate=True).then_inc(negmax_ready, 1)
                elif kind == "PV":
                    u = step[1]
                    t, g, par, half = UNITS[u]
                    b0, n, _ = unit_heads(u)
                    dve.wait_ge(exp_ready, u + 1)
                    own.then(nc.vector.reciprocal(prec[:, u, 0:n], psum_p[:, u, 0:n]))
                    own.settle()
                    src = filled(dve, step)
                    dst = y[:, t, :].rearrange("p (g b z c) -> p g b z c", g=2, z=2, c=HD)[:, g, b0:b0 + n, par, :]
                    nc.vector.tensor_tensor(dst, src[:, 0:HD * n].rearrange("p (j c) -> p j c", j=n),
                                            prec[:, u, 0:n].unsqueeze(2).broadcast_to([P, n, HD]), ALU.mult).then_inc(freed(step), 1)
                elif kind == "scale_y":
                    t = step[1]
                    dve.wait_ge(sq_ready, t + 1)
                    own.then(nc.vector.reciprocal(ystat[:, t, 2, :], ystat[:, t, 1, :]))
                    own.settle()
                    for g in range(2):
                        half = y[:, t, CH * g:CH * g + CH]
                        nc.vector.tensor_scalar(half, half, ystat[:, t, 2, g:g + 1], None, ALU.mult).then_inc(y_normed, 1)
                elif kind == "yT":
                    t, g = step[1:]
                    dve.wait_ge(gnsk_in, 32)
                    src = filled(dve, step)
                    nc.vector.tensor_tensor(yT[t][:, 4 * g:4 * g + 4, :], src[:].rearrange("p (j c) -> p j c", j=4),
                                            gn[:, 4 * g:4 * g + 4].unsqueeze(2).broadcast_to([P, 4, P]),
                                            ALU.mult).then_inc(freed(step), 1)
                elif kind == "ln1a":
                    t = step[1]
                    dve.wait_ge(x_in, 16)
                    f = [(bank[PLACE[("wo", t, n)][0]][:], (bank_full[PLACE[("wo", t, n)][0]], PLACE[("wo", t, n)][1] + 1),
                          (bank_free[PLACE[("wo", t, n)][0]], PLACE[("wo", t, n)][1] + 1)) for n in range(2)]
                    add_residual(t, mod[:, G1, :], f, x[:, t, :], x[:, t, :])
                elif kind == "ln1b":
                    t = step[1]
                    dve.wait_ge(rows2_ready, 1)
                    centre(t, x[:, t, :], mod[:, SC2, :], h2[:, t, :])
                    inverse(t)
                    scale(t, h2[:, t, :], mod[:, SH2, :], h2[:, t, :]).then_inc(h2_ready, 1)
                    dve.wait_ge(h2_ready, t + 1)
                elif kind == "x1":
                    t = step[1]
                    filled(dve, ("PV", len(UNITS) - 1))
                    centre(t, x[:, t, :], lnw[:, 0, :], V_x1[:, t, :])
                    own.then(scale(t, V_x1[:, t, :], lnw[:, 1, :], V_x1[:, t, :]))
                elif kind == "route":
                    head = step[1]
                    dve.wait_ge(consts_in, 16)
                    for z in range(2):
                        settle_bank(dve, ("s", 0, head // 2, z))
                    before = own.n
                    route(head // 2, scores[:, 0, head], head % 2)
                    route_steps = own.n - before
                elif kind == "dots":
                    dots(0, 0, step[1], step[1] + 1)

            for t in range(NT):
                for i in range(4):
                    for z in range(2):
                        settle_bank(dve, ("s", t, i, z))
            base = own.n - 2 * route_steps

            flat = H_s[:].rearrange("p (g z n) -> p g z n", z=2, n=NK)

            def scores_of(head):
                return flat[:, bass.ds(head, 1)].rearrange("p g z n -> p (g z) n")

            def turn_body(turn, t, between):
                for p in range(PAIR // 2):
                    if p in between:
                        between[p]()
                    dots(turn, t, p, p + 1)

            def routes(turn, p0, p1):
                return {p0: lambda: route(turn + 1, scores_of(2 * turn + 2), 0),
                        p1: lambda: route(turn + 1, scores_of(2 * turn + 3), 1)}

            def ln2a(t):
                f = [(tile_sum(t)[n], (f_ready, t + 1), (f_taken, 2 * t + n + 1)) for n in range(2)]
                add_residual(NT + t, mod[:, G2, :], f, V_x1[:, t, :], V_x1[:, t, :])

            def ln2b(t):
                centre(NT + t, V_x1[:, t, :], lnw[:, 2, :], h2[:, t, :])
                inverse(NT + t)
                for n in range(2):
                    half = slice(CH * n, CH * n + CH)
                    scale(NT + t, h2[:, t, half], lnw[:, 3, half], V_x1[:, t, half]).then_inc(out_ready, 1)

            with dve.Fori(1, TURNS) as turn:
                own.n = turn * (2 * route_steps) + base
                turn_body(turn, 0, routes(turn, *ROUTE_AT))
            own.n = base + TURNS * 2 * route_steps
            dve.wait_ge(x1_ready, 1)
            turn_body(TURNS, 1, {LN2_AT[0]: lambda: ln2a(0), LN2_AT[1]: lambda: ln2b(0)} | routes(TURNS, *ROUTE_LATE_AT))
            base = own.n - (TURNS + 1) * 2 * route_steps
            with dve.Fori(TURNS + 1, NT * TURNS - 1) as turn:
                own.n = turn * (2 * route_steps) + base
                turn_body(turn, 1, routes(turn, *ROUTE_AT))
            own.n = base + (NT * TURNS - 1) * 2 * route_steps
            turn_body(NT * TURNS - 1, 1, {})
            ln2a(1)
            ln2b(1)

        @block.gpsimd
        def _(pool):
            own = Steps(pool, pool_step)
            pool.wait_ge(ln_in, 16)
            for m in range(2, 6):
                settle_bank(pool, ("modrow", m))
            filled(pool, ("tflip", 7))
            own.then(nc.gpsimd.tensor_tensor(H_s[:, 0:D], lnw[:, 1, :], mod[:, SC2, :], ALU.mult))
            own.settle()
            own.then(nc.gpsimd.tensor_tensor(mod[:, SH2, :], mod[:, SH2, :], H_s[:, 0:D], ALU.add))
            own.then(nc.gpsimd.tensor_tensor(mod[:, SC2, :], mod[:, SC2, :], lnw[:, 0, :], ALU.mult))
            own.settle()
            pool.sem_inc(rows2_ready, 1)
            pool.wait_ge(inverse_ready, 1)
            filled(pool, ("PV", len(UNITS) - 1))
            own.then(nc.gpsimd.tensor_scalar(V_x1[:, 0, :], x[:, 0, :], lnst[:, 0, 2:3], lnst[:, 0, 5:6], ALU.add, ALU.mult))
            own.settle()
            own.then(nc.gpsimd.tensor_tensor(V_x1[:, 0, :], V_x1[:, 0, :], lnw[:, 0, :], ALU.mult))
            own.settle()
            nc.gpsimd.tensor_tensor(V_x1[:, 0, :], V_x1[:, 0, :], lnw[:, 1, :], ALU.add).then_inc(x1_ready, 1)

            with pool.Fori(0, NT * TURNS) as turn:
                for h in range(2):
                    pool.wait_ge(e_ready, turn * 2 + (h + 1))
                    pool.sem_inc(pool_gate, 1)
                    nc.gpsimd.tensor_copy(idx[:, h, :], e_all[:, bass.ds(turn * PAIR + TOPK * h, TOPK)]).then_inc(idx_staged, 1)
                    pool.wait_ge(idx_staged, turn * 2 + (h + 1))
                    pool.sem_inc(pool_gate, 1)
                    for k in range(TOPK):
                        s = TOPK * h + k
                        r = SLOT_PLACES[s % RING]
                        pool.wait_ge(slot_free, turn * PAIR + (s + 1))
                        pool.sem_inc(pool_gate, 1)
                        nc.gpsimd.indirect_dma_start(ring[:, r, :], None, A["experts"],
                                                     bass.IndirectOffsetOnAxis(ap=idx[:, h, k:k + 1], axis=0)).then_inc(slot_in[r], 16)


def shape_constants():
    dist = (T - 1) - np.arange(ROW)
    n = np.maximum(dist, 1).astype(np.float32)
    large = BUCKETS // 2 + (np.log(n / 16) / math.log(2048 / 16) * 16).astype(np.int32)
    bucket = np.where(dist < 16, np.maximum(dist, 0), np.minimum(large, BUCKETS - 1))
    onehot = ((np.arange(BUCKETS)[:, None] == bucket) & (dist >= 0)).astype(np.float32)
    times = sum(((dist % d == 0) & (dist >= 0) & (dist <= w)).astype(np.int32) for w, d in ((128, 1), (512, 4), (2048, 16)))
    moba = np.where(dist >= 0, 0.0, MASKED)
    dil = np.where(times > 0, np.log(np.maximum(times, 1)), MASKED)
    maskrow = np.concatenate([np.tile(moba, (NH // 2, 1)), np.tile(dil, (NH // 2, 1))]).astype(np.float32)
    consts = np.concatenate([np.eye(P), np.eye(P)[::-1], np.tile(np.arange(TOPK), (P, 1))], 1).astype(np.float32)
    return onehot, maskrow, consts


def kernel(**inputs):
    import concourse.bacc as bacc
    from concourse.bass_utils import run_bass_kernel_spmd

    a = {k: np.asarray(v) for k, v in inputs.items()}

    def columns(v):
        return v.reshape(-1, P).T

    def chunks(w):
        return w.reshape(KC, P, -1, CH).transpose(2, 1, 0, 3).reshape(-1, P, KC * CH)

    w = {"ada": chunks(a["w_ada"][0]), "in": chunks(a["w_in"][0]), "out": chunks(a["w_out"][0]), "q": chunks(a["w_q_peer"][0])}
    order = [8 * g + 2 * b + par for g in range(2) for par in range(2) for b in range(4)]
    onehot, maskrow, consts = shape_constants()
    arrays = {
        "c": columns(a["c"][0]),
        "b_ada_c": columns(a["b_ada"][0, :2 * D]),
        "b_ada_r": a["b_ada"][:, 2 * D:],
        "w": np.stack([w[m][c] for m, c in STREAM]),
        "xT": a["x"][0].T.reshape(KC, P, T).transpose(1, 0, 2).reshape(P, KC * T),
        "x": a["x"][0],
        "ln": np.concatenate([a["ln1_g"], a["ln1_b"], a["ln2_g"], a["ln2_b"]], 1),
        "gn": columns(np.concatenate([a["gn_moba"][0], a["gn_dil"][0]])),
        "skT": a["sub_keys"][0].transpose(0, 2, 1).reshape(P, NK),
        "relT": a["rel_bias"][order].T,
        "experts": np.concatenate([a["peer_u"][0], a["peer_v"][0]], 1),
        "onehot": onehot, "maskrow": maskrow, "consts": consts,
    }
    nc = bacc.Bacc("TRN2", target_bir_lowering=False, num_devices=1)
    feeds, A = {}, {}
    for name, v in arrays.items():
        v = np.ascontiguousarray(v)
        feeds[f"in_{name}"] = v
        A[name] = nc.dram_tensor(f"in_{name}", v.shape, mybir.dt.from_np(v.dtype), kind="ExternalInput").ap()
    A["scratch"] = nc.dram_tensor("scratch", (NH, ROW), F32, kind="Internal").ap()
    out = nc.dram_tensor("out_x", (1, T, D), F32, kind="ExternalOutput").ap()
    build(nc, A, out)
    r = run_bass_kernel_spmd(nc, [feeds], core_ids=[0])
    return r.results[0]["out_x"]
```
